# Optimizing a Trainium2 kernel written in Bass

```python
import jax, jax.numpy as jnp
from jax import lax
import numpy as np
import math

D_MODEL = 2048
BATCH = 1
SEQ = 256
DEPTH = 1

CHUNK = 64
HG_HEADS = 8
HG_DK = 128
HG_DV = 128
HG_WIDTH = HG_HEADS * HG_DV
AT_HEADS = 16
AT_DH = 64
AT_WIDTH = AT_HEADS * AT_DH
LEFT_CHUNKS = 8
BAND = (LEFT_CHUNKS + 1) * CHUNK
REL_CLIP = 256
N_REL = 2 * REL_CLIP + 1
D_FF = 4 * D_MODEL
N_BRANCH = 2
EPS = 1e-6
D_IN = 4 * HG_WIDTH + 3 * AT_WIDTH + N_BRANCH * D_MODEL
SPLIT_POINTS = (HG_WIDTH, 2 * HG_WIDTH, 3 * HG_WIDTH, 4 * HG_WIDTH,
                4 * HG_WIDTH + AT_WIDTH, 4 * HG_WIDTH + 2 * AT_WIDTH, 4 * HG_WIDTH + 3 * AT_WIDTH)


def rms_norm(x, w):
    xf = x.astype(jnp.float32)
    y = xf * lax.rsqrt(jnp.mean(xf * xf, axis=-1, keepdims=True) + EPS)
    return (y * w.astype(jnp.float32)).astype(x.dtype)

def hgrn2_scan(q, k, v, log_g):
    B, H, T, DK = q.shape
    DV = v.shape[-1]
    nc = T // CHUNK

    def to_chunks(a):
        return a.reshape(B, H, nc, CHUNK, a.shape[-1]).transpose(2, 0, 1, 3, 4)

    causal = jnp.tril(jnp.ones((CHUNK, CHUNK), dtype=bool))

    def step(S, inp):
        qc, kc, vc, gc = inp
        b = jnp.cumsum(gc, axis=2)
        o_inter = jnp.einsum('bhtk,bhkv->bhtv', qc * jnp.exp(b), S)
        diff = b[:, :, :, None, :] - b[:, :, None, :, :]
        decay = jnp.exp(jnp.where(causal[:, :, None], diff, -jnp.inf))
        scores = jnp.einsum('bhtk,bhtsk,bhsk->bhts', qc, decay, kc)
        o_intra = jnp.einsum('bhts,bhsv->bhtv', scores, vc)
        b_last = b[:, :, -1:, :]
        S_new = jnp.exp(b_last[:, :, 0, :])[..., None] * S + jnp.einsum(
            'bhsk,bhsv->bhkv', kc * jnp.exp(b_last - b), vc)
        return S_new, o_inter + o_intra

    S0 = jnp.zeros((B, H, DK, DV), jnp.float32)
    _, o = lax.scan(step, S0, (to_chunks(q), to_chunks(k), to_chunks(v), to_chunks(log_g)))
    return o.transpose(1, 2, 0, 3, 4).reshape(B, H, T, DV)

def chunk_band_attention(q, k, v, rel_bias):
    B, H, T, Dh = q.shape
    nc = T // CHUNK
    pad = LEFT_CHUNKS * CHUNK
    kp = jnp.pad(k, ((0, 0), (0, 0), (pad, 0), (0, 0)))
    vp = jnp.pad(v, ((0, 0), (0, 0), (pad, 0), (0, 0)))
    idx = (jnp.arange(nc) * CHUNK)[:, None] + jnp.arange(BAND)[None, :]
    kb = kp[:, :, idx, :]
    vb = vp[:, :, idx, :]
    qc = q.reshape(B, H, nc, CHUNK, Dh)
    valid = idx >= pad
    t = jnp.arange(CHUNK)
    j = jnp.arange(BAND)
    rel = t[:, None] + pad - j[None, :]
    rel_idx = jnp.clip(rel, -REL_CLIP, REL_CLIP) + REL_CLIP
    bias = rel_bias[:, rel_idx].astype(jnp.float32)
    s = jnp.einsum('bhnqd,bhnkd->bhnqk', qc, kb).astype(jnp.float32) * (Dh ** -0.5) + bias[:, None]
    s = jnp.where(valid[:, None, :], s, -jnp.inf)
    p = jax.nn.softmax(s, axis=-1).astype(v.dtype)
    o = jnp.einsum('bhnqk,bhnkd->bhnqd', p, vb)
    return o.reshape(B, H, T, Dh)

def mixer_block(u, w_in, lb, hg_norm_w, rel_bias, w_branch_a, w_branch_b, w_out):
    B, T, _ = u.shape
    z = u @ w_in
    hq, hf, hi, hg, aq, ak, av, gates = jnp.split(z, SPLIT_POINTS, axis=-1)

    def to_heads(a, h):
        return a.reshape(B, T, h, -1).transpose(0, 2, 1, 3)

    f = jax.nn.sigmoid(hf.astype(jnp.float32))
    g = lb + (1.0 - lb) * f
    log_g = jnp.log(g)
    kk = 1.0 - g
    q = jax.nn.silu(hq.astype(jnp.float32)) * (HG_DK ** -0.5)
    o = hgrn2_scan(to_heads(q, HG_HEADS), to_heads(kk, HG_HEADS),
                   to_heads(hi.astype(jnp.float32), HG_HEADS), to_heads(log_g, HG_HEADS))
    o = o.transpose(0, 2, 1, 3)
    o = rms_norm(o, hg_norm_w) * jax.nn.silu(hg.reshape(B, T, HG_HEADS, HG_DV).astype(jnp.float32))
    y_a = o.reshape(B, T, HG_WIDTH).astype(u.dtype)

    ya = chunk_band_attention(to_heads(aq, AT_HEADS), to_heads(ak, AT_HEADS),
                              to_heads(av, AT_HEADS), rel_bias)
    y_b = ya.transpose(0, 2, 1, 3).reshape(B, T, AT_WIDTH)

    gate_a, gate_b = jnp.split(jax.nn.sigmoid(gates), 2, axis=-1)
    merged = gate_a * (y_a @ w_branch_a) + gate_b * (y_b @ w_branch_b)
    return merged @ w_out

def first_inputs(seed: int = 0) -> dict:
    key = jax.random.key(seed)
    ks = jax.random.split(key, 13)
    f32 = jnp.float32
    x = jax.random.normal(ks[0], (BATCH, SEQ, D_MODEL), f32)
    w_in = jax.random.normal(ks[1], (DEPTH, D_MODEL, D_IN), f32) * D_MODEL ** -0.5
    lb_logits = jax.random.normal(ks[2], (DEPTH + 1, HG_WIDTH), f32)
    hg_norm_w = 1.0 + 0.02 * jax.random.normal(ks[3], (DEPTH, HG_DV), f32)
    rel_bias = 0.1 * jax.random.normal(ks[4], (DEPTH, AT_HEADS, N_REL), f32)
    w_branch_a = jax.random.normal(ks[5], (DEPTH, HG_WIDTH, D_MODEL), f32) * HG_WIDTH ** -0.5
    w_branch_b = jax.random.normal(ks[6], (DEPTH, AT_WIDTH, D_MODEL), f32) * AT_WIDTH ** -0.5
    w_out = jax.random.normal(ks[7], (DEPTH, D_MODEL, D_MODEL), f32) * D_MODEL ** -0.5
    norm_mix_w = 1.0 + 0.02 * jax.random.normal(ks[8], (DEPTH, D_MODEL), f32)
    norm_mlp_w = 1.0 + 0.02 * jax.random.normal(ks[9], (DEPTH, D_MODEL), f32)
    w_up = jax.random.normal(ks[10], (DEPTH, D_MODEL, D_FF), f32) * D_MODEL ** -0.5
    w_down = jax.random.normal(ks[11], (DEPTH, D_FF, D_MODEL), f32) * D_FF ** -0.5
    norm_final_w = 1.0 + 0.02 * jax.random.normal(ks[12], (D_MODEL,), f32)
    return {"x": x, "w_in": w_in, "lb_logits": lb_logits, "hg_norm_w": hg_norm_w,
            "rel_bias": rel_bias, "w_branch_a": w_branch_a, "w_branch_b": w_branch_b,
            "w_out": w_out, "norm_mix_w": norm_mix_w, "norm_mlp_w": norm_mlp_w,
            "w_up": w_up, "w_down": w_down, "norm_final_w": norm_final_w}

def first_block(x, w_in, lb_logits, hg_norm_w, rel_bias, w_branch_a, w_branch_b, w_out,
              norm_mix_w, norm_mlp_w, w_up, w_down, norm_final_w):
    lb_all = jnp.cumsum(jax.nn.softmax(lb_logits.astype(jnp.float32), axis=0), axis=0)
    h = x
    for l in range(DEPTH):
        h = h + mixer_block(rms_norm(h, norm_mix_w[l]), w_in[l], lb_all[l], hg_norm_w[l],
                            rel_bias[l], w_branch_a[l], w_branch_b[l], w_out[l])
        u = rms_norm(h, norm_mlp_w[l])
        h = h + jnp.square(jax.nn.relu(u @ w_up[l])) @ w_down[l]
    return rms_norm(h, norm_final_w)


N_META = 16
GRID_W = 64
Q_BLOCK = 128
HEAD_DIM = 128
MIX_WIDTH = D_MODEL
A_WIDTH = MIX_WIDTH // 2
A_HEADS = A_WIDTH // HEAD_DIM
A_KV_HEADS = 2
A_GROUP = A_HEADS // A_KV_HEADS
B_WIDTH = MIX_WIDTH - A_WIDTH
B_V_DIM = HEAD_DIM
B_QK_DIM = HEAD_DIM // 2
B_HEADS = B_WIDTH // B_V_DIM

ROPE_THETA = 10000.0
NORM_EPS = 1e-6

A_Q_COLS = A_HEADS * HEAD_DIM
A_KV_COLS = A_KV_HEADS * HEAD_DIM
A_GATE_COLS = A_WIDTH
B_QK_COLS = B_HEADS * 2 * B_QK_DIM
B_V_COLS = B_HEADS * B_V_DIM
B_GATE_COLS = B_WIDTH
IN_PROJ_SIZES = (A_Q_COLS, A_KV_COLS, A_KV_COLS, A_GATE_COLS,
                 B_QK_COLS, B_QK_COLS, B_V_COLS, B_GATE_COLS)
IN_PROJ_WIDTH = sum(IN_PROJ_SIZES)
SPLIT_POINTS_2 = tuple(int(c) for c in np.cumsum(IN_PROJ_SIZES)[:-1])


def rmsnorm(x, g):
    xf = x.astype(jnp.float32)
    r = lax.rsqrt(jnp.mean(xf * xf, axis=-1, keepdims=True) + NORM_EPS)
    return (xf * r * g.astype(jnp.float32)).astype(x.dtype)

def alibi_slopes(n_heads):
    return 2.0 ** (-8.0 * (jnp.arange(n_heads, dtype=jnp.float32) + 1.0) / n_heads)

def axial_angles(grid_pos):
    axis_dim = HEAD_DIM // 2
    inv_freq = ROPE_THETA ** (-jnp.arange(0, axis_dim, 2, dtype=jnp.float32) / axis_dim)
    return grid_pos.astype(jnp.float32)[:, None] * inv_freq[None, :]

def rope_half(x, ang):
    x1, x2 = jnp.split(x, 2, axis=-1)
    c, s = jnp.cos(ang), jnp.sin(ang)
    return jnp.concatenate([x1 * c - x2 * s, x2 * c + x1 * s], axis=-1)

def axial_rope(x, ang_row, ang_col):
    xf = x.astype(jnp.float32)
    xr, xc = jnp.split(xf, 2, axis=-1)
    return jnp.concatenate([rope_half(xr, ang_row), rope_half(xc, ang_col)], axis=-1).astype(x.dtype)

def sweep_query_blocks(attend, qs, qpos):
    meta_out = attend(tuple(q[..., :N_META, :] for q in qs), qpos[:N_META])
    n_real = qpos.shape[0] - N_META
    n_blk = n_real // Q_BLOCK

    def to_blocks(a):
        a = a[..., N_META:, :]
        a = a.reshape(a.shape[:-2] + (n_blk, Q_BLOCK, a.shape[-1]))
        return jnp.moveaxis(a, -3, 0)

    blk_q = tuple(to_blocks(q) for q in qs)
    blk_pos = qpos[N_META:].reshape(n_blk, Q_BLOCK)
    out = lax.map(lambda args: attend(args[0], args[1]), (blk_q, blk_pos))
    out = jnp.moveaxis(out, 0, -3)
    out = out.reshape(out.shape[:-3] + (n_real, out.shape[-1]))
    return jnp.concatenate([meta_out, out], axis=-2)

def heads_first(t, n_heads, d):
    b, l, _ = t.shape
    return t.reshape(b, l, n_heads, d).transpose(0, 2, 1, 3)

def gqa_axial_mixer(qa, ka, va, q_g, k_g, ang_row, ang_col, pos):
    b, l, _ = qa.shape
    q = axial_rope(rmsnorm(heads_first(qa, A_HEADS, HEAD_DIM), q_g), ang_row, ang_col)
    k = axial_rope(rmsnorm(heads_first(ka, A_KV_HEADS, HEAD_DIM), k_g), ang_row, ang_col)
    v = heads_first(va, A_KV_HEADS, HEAD_DIM)
    q = q.reshape(b, A_KV_HEADS, A_GROUP, l, HEAD_DIM)
    scale = 1.0 / math.sqrt(HEAD_DIM)

    def attend(qs, qpos):
        s = jnp.einsum('bkgqd,bksd->bkgqs', qs[0], k).astype(jnp.float32) * scale
        p = jax.nn.softmax(s, axis=-1)
        return jnp.einsum('bkgqs,bksd->bkgqd', p.astype(v.dtype), v)

    o = sweep_query_blocks(attend, (q,), pos)
    return o.transpose(0, 3, 1, 2, 4).reshape(b, l, A_WIDTH)

def diff_attn_mixer(qb, kb, vb, lq1, lk1, lq2, lk2, sub_g, lambda_init, pos):
    b, l, _ = qb.shape
    q = qb.reshape(b, l, B_HEADS, 2, B_QK_DIM).transpose(0, 2, 3, 1, 4)
    k = kb.reshape(b, l, B_HEADS, 2, B_QK_DIM).transpose(0, 2, 3, 1, 4)
    q1, q2 = q[:, :, 0], q[:, :, 1]
    k1, k2 = k[:, :, 0], k[:, :, 1]
    v = heads_first(vb, B_HEADS, B_V_DIM)
    lam = (jnp.exp(jnp.sum(lq1.astype(jnp.float32) * lk1.astype(jnp.float32)))
           - jnp.exp(jnp.sum(lq2.astype(jnp.float32) * lk2.astype(jnp.float32)))
           + lambda_init)
    slopes = alibi_slopes(B_HEADS)
    kpos = pos.astype(jnp.float32)
    scale = 1.0 / math.sqrt(B_QK_DIM)

    def attend(qs, qpos):
        dist = jnp.abs(qpos.astype(jnp.float32)[:, None] - kpos[None, :])
        bias = -slopes[:, None, None] * dist[None]
        s1 = jnp.einsum('bhqd,bhkd->bhqk', qs[0], k1).astype(jnp.float32) * scale + bias
        s2 = jnp.einsum('bhqd,bhkd->bhqk', qs[1], k2).astype(jnp.float32) * scale + bias
        a = jax.nn.softmax(s1, axis=-1) - lam * jax.nn.softmax(s2, axis=-1)
        return jnp.einsum('bhqk,bhkd->bhqd', a.astype(v.dtype), v)

    o = sweep_query_blocks(attend, (q1, q2), pos)
    o = rmsnorm(o, sub_g) * (1.0 - lambda_init)
    return o.transpose(0, 2, 1, 3).reshape(b, l, B_WIDTH)

def second_inputs(seed: int = 0) -> dict:
    key = jax.random.key(seed)
    ks = jax.random.split(key, 13)
    f32 = jnp.float32
    return {
        "x": jax.random.normal(ks[0], (BATCH, SEQ, D_MODEL), f32),
        "meta_tokens": jax.random.normal(ks[1], (N_META, D_MODEL), f32),
        "pre_norm_g": 1.0 + 0.02 * jax.random.normal(ks[2], (DEPTH, D_MODEL), f32),
        "w_in": jax.random.normal(ks[3], (DEPTH, D_MODEL, IN_PROJ_WIDTH), f32) * D_MODEL ** -0.5,
        "q_norm_g": 1.0 + 0.02 * jax.random.normal(ks[4], (DEPTH, HEAD_DIM), f32),
        "k_norm_g": 1.0 + 0.02 * jax.random.normal(ks[5], (DEPTH, HEAD_DIM), f32),
        "lambda_q1": 0.1 * jax.random.normal(ks[6], (DEPTH, B_QK_DIM), f32),
        "lambda_k1": 0.1 * jax.random.normal(ks[7], (DEPTH, B_QK_DIM), f32),
        "lambda_q2": 0.1 * jax.random.normal(ks[8], (DEPTH, B_QK_DIM), f32),
        "lambda_k2": 0.1 * jax.random.normal(ks[9], (DEPTH, B_QK_DIM), f32),
        "subln_g": 1.0 + 0.02 * jax.random.normal(ks[10], (DEPTH, B_V_DIM), f32),
        "w_out": jax.random.normal(ks[11], (DEPTH, MIX_WIDTH, D_MODEL), f32) * MIX_WIDTH ** -0.5,
        "post_norm_g": 1.0 + 0.02 * jax.random.normal(ks[12], (DEPTH, D_MODEL), f32),
    }

def second_block(x, meta_tokens, pre_norm_g, w_in, q_norm_g, k_norm_g, lambda_q1, lambda_k1,
              lambda_q2, lambda_k2, subln_g, w_out, post_norm_g):
    b, n_real, _ = x.shape
    meta = jnp.broadcast_to(meta_tokens.astype(x.dtype)[None], (b, N_META, D_MODEL))
    h = jnp.concatenate([meta, x], axis=1)
    seq_len = N_META + n_real
    pos = jnp.arange(seq_len, dtype=jnp.int32)

    rows = n_real // GRID_W
    grid_row = jnp.concatenate([jnp.zeros((N_META,), jnp.int32),
                                jnp.repeat(jnp.arange(rows, dtype=jnp.int32), GRID_W)])
    grid_col = jnp.concatenate([jnp.zeros((N_META,), jnp.int32),
                                jnp.tile(jnp.arange(GRID_W, dtype=jnp.int32), rows)])
    ang_row = axial_angles(grid_row)
    ang_col = axial_angles(grid_col)

    for layer in range(DEPTH):
        lambda_init = 0.8 - 0.6 * math.exp(-0.3 * layer)
        hn = rmsnorm(h, pre_norm_g[layer])
        proj = jnp.einsum('bld,dc->blc', hn, w_in[layer])
        qa, ka, va, ga, qb, kb, vb, gb = jnp.split(proj, SPLIT_POINTS_2, axis=-1)
        ya = gqa_axial_mixer(qa, ka, va, q_norm_g[layer], k_norm_g[layer],
                             ang_row, ang_col, pos) * jax.nn.silu(ga)
        yb = diff_attn_mixer(qb, kb, vb, lambda_q1[layer], lambda_k1[layer], lambda_q2[layer],
                             lambda_k2[layer], subln_g[layer], lambda_init, pos) * jax.nn.silu(gb)
        y = jnp.einsum('blc,cd->bld', jnp.concatenate([ya, yb], axis=-1), w_out[layer])
        h = h + rmsnorm(y, post_norm_g[layer])

    return h[:, N_META:, :]


def setup_inputs(seed=0):
    out = dict(first_inputs(seed))
    for name, value in second_inputs(seed + 1).items():
        if name != "x":
            out[name + "_2"] = value
    return out


def reference(
    x, w_in, lb_logits, hg_norm_w, rel_bias, w_branch_a, w_branch_b, w_out, norm_mix_w,
    norm_mlp_w, w_up, w_down, norm_final_w, meta_tokens_2, pre_norm_g_2, w_in_2, q_norm_g_2,
    k_norm_g_2, lambda_q1_2, lambda_k1_2, lambda_q2_2, lambda_k2_2, subln_g_2, w_out_2,
    post_norm_g_2,
):
    x = first_block(
        x, w_in, lb_logits, hg_norm_w, rel_bias, w_branch_a, w_branch_b, w_out, norm_mix_w,
        norm_mlp_w, w_up, w_down, norm_final_w,
    )
    return second_block(
        x, meta_tokens_2, pre_norm_g_2, w_in_2, q_norm_g_2, k_norm_g_2, lambda_q1_2,
        lambda_k1_2, lambda_q2_2, lambda_k2_2, subln_g_2, w_out_2, post_norm_g_2,
    )


_drawn_inputs = setup_inputs


def setup_inputs(seed=0):
    import zlib

    import numpy as np

    out = dict(_drawn_inputs(seed))
    spreads = {}
    factors = {'hg_norm_w': 6.973,
     'rel_bias': 6.157,
     'norm_mix_w': 4.584,
     'norm_mlp_w': 2.704,
     'q_norm_g_2': 8.0,
     'k_norm_g_2': 8.0,
     'lambda_q1_2': 3.106,
     'subln_g_2': 4.403,
     'post_norm_g_2': 3.845}
    for name, (base, spread) in spreads.items():
        noise = np.random.default_rng([zlib.crc32(name.encode()), seed]).standard_normal(out[name].shape)
        drawn = base * np.exp(spread * noise) if base else spread * noise
        out[name] = __import__('jax').numpy.asarray(drawn.astype(out[name].dtype))
    for name, factor in factors.items():
        out[name] = (out[name] * factor).astype(out[name].dtype)
    return out
```

```python
import math
from contextlib import ExitStack

import numpy as np

import concourse.bass as bass
from concourse import mybir

ACT = mybir.ActivationFunctionType
ALU = mybir.AluOpType
AX = mybir.AxisListType
F32 = mybir.dt.float32
F32R = mybir.dt.float32r

P = 128
D = 2048
T = 256
NT = T // P
META = 16
TM = T + META
KT = D // P
HG = 8
AH = 16
DH = 64
N_REL = 513
REL_CLIP = 256
H2 = 8
KV2 = 2
EPS = 1e-6
MASKED = -1e30

CW = 512
CK = 2
NC = KT // CK
SLOTS = 4
LEAD = 4

C_IN = 0
G_IN = 22
C_BR = C_IN + G_IN * NC
C_OUT = C_BR + 4 * NC
C_FF = C_OUT + 4 * NC
QUARTERS = 4
C_IN2 = C_FF + QUARTERS * 8 * NC
IN2_COLS = (3584, 4096, 4608, 5120, 1024, 2560, 3072, 0, 512, 5632, 6144, 1536, 2048)
G_IN2 = len(IN2_COLS)
C_OUT2 = C_IN2 + G_IN2 * NC
C_END = C_OUT2 + 4 * NC
SETS_BEFORE_2 = (G_IN + 8 + 4 + 32) // 2

LEVELS = 9
G_LEVEL = 5
G_HGOUT = G_LEVEL + LEVELS
G_ATT = 16
J_B = 6
B_UNITS = H2 * NT
B_SLOTS = B_UNITS + 3
A_UNITS = H2 * NT
A_SLOTS = A_UNITS + 4
POS_A = 2 * B_SLOTS
POS_BN = POS_A + 1

LAMBDA_INIT = 0.8 - 0.6 * math.exp(-0.3 * 0)
N_CONST = 16
E_STEP = {g: n for n, g in enumerate([0, 1, 2, 3, 6, 7])}
N_E1 = len(E_STEP)


def program(nc, x, w_in, lb_logits, hg_norm_w, rel_bias, w_branch_a, w_branch_b, w_out, norm_mix_w,
            norm_mlp_w, w_up, w_down, norm_final_w, meta_tokens_2, pre_norm_g_2, w_in_2, q_norm_g_2,
            k_norm_g_2, lambda_q1_2, lambda_k1_2, lambda_q2_2, lambda_k2_2, subln_g_2, w_out_2,
            post_norm_g_2, identity, level_masks, rope_cos, rope_sin, rope_turn, distance, out):
    with ExitStack() as ctx:
        def sb(name, shape, dt=F32):
            return ctx.enter_context(nc.sbuf_tensor(name, shape, dt))

        def sem(name):
            return ctx.enter_context(nc.semaphore(name))

        raw = sb("raw", [P, SLOTS, CK, CW])
        whi = sb("whi", [P, SLOTS, CK, CW], F32R)
        wlo = sb("wlo", [P, SLOTS, CK, CW], F32R)
        xhi = sb("xhi", [P, KT, TM], F32R)
        xlo = sb("xlo", [P, KT, TM], F32R)
        ident = sb("ident", [P, P])
        ones = sb("ones", [P, P])
        mix_w = sb("mix_w", [P, KT])
        mlp_w = sb("mlp_w", [P, KT])
        pre_w = sb("pre_w", [P, KT])
        lbt = sb("lbt", [P, 2, HG])
        lbe = sb("lbe", [P, 2, HG])
        lbs = sb("lbs", [P, 4, HG])
        gvec = sb("gvec", [P, 4])
        subg = sb("subg", [P, 1])
        lamv = sb("lamv", [P, 4, DH])
        lams = sb("lams", [P, 8])
        eps_t = sb("eps_t", [P, 1])
        ss = sb("ss", [P, 16])
        sq = sb("sq", [P, 3, NT, 4])
        rstd = sb("rstd", [P, 16])
        nm = sb("nm", [P, 4, 2])
        rsum = sb("rsum", [P, 4, 2])
        rinv = sb("rinv", [P, 4, 2])
        cos_t = sb("cos_t", [P, TM])
        sin_t = sb("sin_t", [P, TM])
        turn = sb("turn", [P, P])
        dist = sb("dist", [P, NT, TM])
        ps = ctx.enter_context(nc.psum_tensor("ps", [P, 8, 512], F32))

        def at(name, kib, shape, dt=F32):
            with ExitStack() as tmp:
                if kib:
                    tmp.enter_context(nc.sbuf_tensor(name + "_pad", [P, int(kib * 256)], F32))
                return tmp.enter_context(nc.sbuf_tensor(name, shape, dt))

        x_nat = at("x_nat", 32, [P, NT, D])
        meta_nat = at("meta_nat", 80, [META, D])
        junk = at("junk", 72, [P, D])
        junk_b = at("junk_b", 108, [P, D])
        junk3 = at("junk3", 56, [P, D])
        junk3_b = at("junk3_b", 64, [P, D])
        meta_t = at("meta_t", 88, [P, KT, META])
        qp = at("qp", 16, [P, HG, T])
        v_hg = at("v_hg", 24, [P, NT, HG * P])
        aq = at("aq", 32, [P, HG, T])
        ak = at("ak", 40, [P, HG, T])
        av = at("av", 48, [P, NT, AH * DH])
        g_even = at("g_even", 56, [P, HG * T])
        g_odd = at("g_odd", 64, [P, HG * T // 2])
        cross = at("cross", 56, [P, HG, P])
        acc = at("acc", 68, [P, HG * NT, P])
        masked = at("masked", 76, [P, HG * NT, P])
        kr = at("kr", 88, [P, HG, T])
        sg = at("sg", 96, [P, HG, T])
        masks = at("masks", 104, [P, 8, P])
        o_hg = at("o_hg", 88, [P, HG, T])
        o2_hg = at("o2_hg", 76, [P, HG, T])
        rs_hg = at("rs_hg", 80, [P, HG, T])
        ya_hi = at("ya_hi", 0, [P, 8, T], F32R)
        ya_lo = at("ya_lo", 8, [P, 8, T], F32R)
        yb_hi = at("yb_hi", 16, [P, 8, T], F32R)
        yb_lo = at("yb_lo", 24, [P, 8, T], F32R)
        gates = at("gates", 56, [P, 32, T])
        rel = at("rel", 104, [P, 2, 2, T])
        prob = at("prob", 108, [P, 3, 3 * P])
        prob_t = at("prob_t", 112.5, [P, 2, 3 * P])
        part_a = at("part_a", 88, [P, 4, T])
        part_b = at("part_b", 92, [P, 4, T])
        both = at("both", 96, [P, 4, T])
        h = at("h", 32, [P, NT, D])
        normed = at("normed", 56, [P, NT, D])
        relu = at("relu", 88, [P, 4, T])
        relu2 = at("relu2", 96, [P, 4, T])
        fin_w = at("fin_w", 80, [P, D])
        kb = at("kb", 0, [P, H2, TM])
        qb = at("qb", 8.5, [P, H2, T])
        v_nat = at("v_nat", 17, [P, 10, NT, P])
        v_meta = at("v_meta", 27, [META, 10, P])
        ka = at("ka", 48, [P, KV2, TM])
        qa = at("qa", 51, [P, H2, T])
        v_t = at("v_t", 60, [P, 10, TM])
        oa = at("oa", 60, [P, H2, T])
        ob = at("ob", 68, [P, H2, T])
        pt2 = at("pt2", 76.5, [P, 2, 3 * P])
        ga = at("ga", 80, [P, H2, T])
        gb = at("gb", 88, [P, H2, T])
        qg = at("qg", 96, [P, 4, TM])
        qsq = at("qsq", 100.25, [P, 4, TM])
        qrot = at("qrot", 104.5, [P, 4, TM])
        p2 = at("p2", 108.75, [P, 3, 2, TM])
        ob2 = at("ob2", 0, [P, H2, T])
        obr = at("obr", 8.5, [P, H2, T])
        y2 = at("y2", 0, [P, NT, D])
        post_w = at("post_w", 88, [P, D])
        junk2 = at("junk2", 96, [P, D])

        raw_in = [sem(f"raw_in{i}") for i in range(SLOTS)]
        whi_ready = sem("whi_ready")
        wlo_ready = sem("wlo_ready")
        pe_done = sem("pe_done")
        set_free = [sem(f"set_free{i}") for i in range(2)]
        kvb_free = sem("kvb_free")
        x_in = [sem("x_in0"), sem("x_in1")]
        ident_in, mixw_in, c_in, meta_in = [sem(n) for n in ("ident_in", "mixw_in", "c_in", "meta_in")]
        mask_in, h_in, finw_in, postw_in = [sem(n) for n in ("mask_in", "h_in", "finw_in", "postw_in")]
        rel_in = [sem("rel_in0"), sem("rel_in1")]
        rel_ready = sem("rel_ready")
        n_ss, n_sum, n_sd, n_rs, n_un0, n_un1, n_tr, n_hi = [sem(n) for n in (
            "n_ss", "n_sum", "n_sd", "n_rs", "n_un0", "n_un1", "n_tr", "n_hi")]
        x_ready = sem("x_ready")
        f_w, f_sq, f_un = sem("f_w"), sem("f_sq"), sem("f_un")
        h_ready = sem("h_ready")
        setup = sem("setup")
        lb_max, lb_exp, lam_sum, lam_exp = [sem(n) for n in ("lb_max", "lb_exp", "lam_sum", "lam_exp")]
        m_ss, m_sd, m_un, m_tr, m_hi, meta_ready, m_w = [sem(n) for n in ("m_ss", "m_sd", "m_un", "m_tr", "m_hi", "meta_ready", "m_w")]
        e_sig = sem("e_sig")
        dve_step = sem("dve_step")
        sp_turn = sem("sp_turn")
        pool_step = sem("pool_step")
        hg_s, hg_m, hg_acc, hg_q, hg_k, hg_g = [sem(n) for n in ("hg_s", "hg_m", "hg_acc", "hg_q", "hg_k", "hg_g")]
        hg_o, hg_os, hg_o2, hg_ss, hg_sd, hg_rs, hg_t, hg_y, hg_hi, ya_ready = [sem(n) for n in (
            "hg_o", "hg_os", "hg_o2", "hg_ss", "hg_sd", "hg_rs", "hg_t", "hg_y", "hg_hi", "ya_ready")]
        at_s, at_nm, at_exp, at_p, at_t, at_pt, at_pv, at_hi, at_y = [sem(n) for n in (
            "at_s", "at_nm", "at_exp", "at_p", "at_t", "at_pt", "at_pv", "at_hi", "at_y")]
        br_m, br_hi, br_ready = sem("br_m"), sem("br_hi"), sem("br_ready")
        up_sq, up_hi, up_ready = [sem(n) for n in ("up_sq", "up_hi", "up_ready")]
        vt_t, vt_c = [sem("vt_t0"), sem("vt_t1")], [sem("vt_c0"), sem("vt_c1")]
        nr_ev, nr_ss, nr_sd, nr_rs, nr_rot, nr_sin, nr_cos, nr_done = [sem(n) for n in (
            "nr_ev", "nr_ss", "nr_sd", "nr_rs", "nr_rot", "nr_sin", "nr_cos", "nr_done")]
        b_s, b_nm, b_exp, b_p, b_t, b_pt, b_pv, b_o = [sem(n) for n in (
            "b_s", "b_nm", "b_exp", "b_p", "b_t", "b_pt", "b_pv", "b_o")]
        a_s, a_nm, a_exp, a_p, a_t, a_pt, a_pv, a_o = [sem(n) for n in (
            "a_s", "a_nm", "a_exp", "a_p", "a_t", "a_pt", "a_pv", "a_o")]
        bn_o2, bn_ss, bn_c, bn_sd, bn_rs, bn_y, bn_hi, yb2_ready = [sem(n) for n in (
            "bn_o2", "bn_ss", "bn_c", "bn_sd", "bn_rs", "bn_y", "bn_hi", "yb2_ready")]
        an_y, an_hi, ya2_ready = sem("an_y"), sem("an_hi"), sem("ya2_ready")
        y_ss, y_sd, y_rs, y_n, y_out, stored = [sem(n) for n in ("y_ss", "y_sd", "y_rs", "y_n", "y_out", "stored")]

        def tiles(w, lead=True):
            return (w[0] if lead else w).rearrange("(k p) n -> p k n", p=P)

        w_in_t, w_a_t, w_b_t = tiles(w_in), tiles(w_branch_a), tiles(w_branch_b)
        w_out_t, w_up_t, w_down_t = tiles(w_out), tiles(w_up), tiles(w_down)
        w_in2_t, w_out2_t = tiles(w_in_2), tiles(w_out_2)

        def pset(s):
            return ps[:, 2 * s:2 * s + 2, :].rearrange("p b (x c) -> p (b x) c", x=2)

        misc = ps[:, 4:8, :]

        def spread(a, *dims):
            return bass.AP(a.tensor, a.offset, [list(a.ap[0])] + [list(d) for d in dims])

        def row_all(w, n):
            return bass.AP(w.tensor, w.offset, [[0, P], [1, n]])

        def set_needs():
            n = [SETS_BEFORE_2 + 3] * 2
            need = {}
            for j in range(5, G_IN2):
                s = (j - 5) % 2
                need[j] = n[s]
                n[s] += 1
                if j == 5:
                    n[1] += 1
            return need, n

        need2, sets_before_out2 = set_needs()

        block = ctx.enter_context(nc.Block())

        @block.sync
        def _(sp):
            def chunk(c0, k, src):
                if not isinstance(c0, int) or c0 + k >= SLOTS:
                    sp.wait_ge(wlo_ready, c0 + k - SLOTS + 1)
                    sp.sem_inc(sp_turn, 1)
                sp.dma_start(raw[:, k % SLOTS], src).then_inc(raw_in[k % SLOTS], 16)

            def rows(w, k, cols):
                return w[:, CK * k:CK * k + CK, cols]

            sp.dma_start(ident[:], identity).then_inc(ident_in, 16)
            for t in range(NT):
                sp.dma_start(x_nat[:, t], x[0, t * P:(t + 1) * P, :]).then_inc(x_in[t], 16)
            for k in range(NC):
                chunk(C_IN, k, rows(w_in_t, k, slice(0, CW)))
            with sp.Fori(1, G_IN) as g:
                for k in range(NC):
                    chunk(C_IN + NC * g, k, rows(w_in_t, k, bass.ds(g * CW, CW)))
            sp.wait_ge(at_s, AH)
            sp.dma_start(h[:], x[0].rearrange("(t p) d -> p t d", p=P)).then_inc(h_in, 16)
            with sp.Fori(0, 4) as n:
                for k in range(NC):
                    w = w_a_t if k < NC // 2 else w_b_t
                    chunk(C_BR + NC * n, k, rows(w, k % (NC // 2), bass.ds(n * CW, CW)))
            with sp.Fori(0, 4) as n:
                for k in range(NC):
                    chunk(C_OUT + NC * n, k, rows(w_out_t, k, bass.ds(n * CW, CW)))
            with sp.Fori(0, QUARTERS) as q:
                with sp.Fori(0, 4) as n:
                    for k in range(NC):
                        chunk(C_FF + 8 * NC * q + NC * n, k, rows(w_up_t, k, bass.ds(q * D + n * CW, CW)))
                with sp.Fori(0, 4) as n:
                    for k in range(NC):
                        chunk(C_FF + 8 * NC * q + 4 * NC + NC * n, k,
                              w_down_t[:, bass.ds(q * KT + CK * k, CK), bass.ds(n * CW, CW)])
            for j, col in enumerate(IN2_COLS):
                for k in range(NC):
                    chunk(C_IN2 + NC * j, k, rows(w_in2_t, k, slice(col, col + CW)))
            with sp.Fori(0, 4) as n:
                for k in range(NC):
                    chunk(C_OUT2 + NC * n, k, rows(w_out2_t, (k + NC // 2) % NC, bass.ds(n * CW, CW)))
            for t in range(NT):
                sp.wait_ge(y_out, t + 1)
                sp.dma_start(out[0, t * P:(t + 1) * P, :], y2[:, t]).then_inc(stored, 16)
            sp.wait_ge(stored, 16 * NT)

        @block.tensor
        def _(pe):
            mm = nc.tensor.matmul

            def chunk_t(c0, k, kt0, xh, xl, outs, n, first, last, shared=True):
                pe.wait_ge(wlo_ready, c0 + k + 1)
                for j in range(CK):
                    kt = kt0 + j
                    for b in range(4):
                        cols = slice(b * P, (b + 1) * P)
                        for i, (w, v) in enumerate(((whi, xh), (whi, xl), (wlo, xh))):
                            start = first and j == 0 and i == 0 and (b % 2 == 0 or not shared)
                            ins = mm(outs[b], w[:, k % SLOTS, j, cols], v[:, kt, 0:n], start=start,
                                     stop=last and j == CK - 1 and i == 2, skip_group_check=True)
                ins.then_inc(pe_done, 1)

            def chunk_n(c0, k, kt0, xh, xl, s, first, last):
                pe.wait_ge(wlo_ready, c0 + k + 1)
                for j in range(CK):
                    kt = kt0 + j
                    for t in range(NT):
                        toks = slice(t * P, (t + 1) * P)
                        for i, (v, w) in enumerate(((xh, whi), (xh, wlo), (xl, whi))):
                            ins = mm(ps[:, 2 * s + t, :], v[:, kt, toks], w[:, k % SLOTS, j, :],
                                     start=first and j == 0 and i == 0,
                                     stop=last and j == CK - 1 and i == 2, skip_group_check=True)
                ins.then_inc(pe_done, 1)

            def blocks(s):
                return [pset(s)[:, b, :] for b in range(4)]

            def turn_normed(b):
                for kt in range(KT):
                    if kt % 4 == 0:
                        pe.wait_ge(n_un0, 4 * b + kt // 4 + 1)
                        pe.wait_ge(n_un1, 4 * b + kt // 4 + 1)
                    if kt >= 8 and kt % 2 == 0:
                        pe.wait_ge(x_ready, KT * b + kt - 6)
                    for t in range(NT):
                        o = (kt % 2) * T + t * P
                        ins = nc.tensor.transpose(ps[:, 4 + (kt % 8) // 2, o:o + P],
                                                  normed[:, t, kt * P:(kt + 1) * P], ident[:])
                    if kt % 2 == 1:
                        ins.then_inc(n_tr, 1)

            def turn_meta():
                pe.wait_ge(m_un, 1)
                for kt in range(KT):
                    ins = nc.tensor.transpose(ps[:, 3, kt * META:(kt + 1) * META],
                                              meta_nat[:, kt * P:(kt + 1) * P], ident[0:META, 0:META])
                ins.then_inc(m_tr, 1)

            pe.wait_ge(ident_in, 16)
            turn_normed(0)

            def level_scores(level):
                pe.wait_ge(hg_m, 2 * level) if level else None
                if level:
                    pe.wait_ge(hg_q, level)
                if level > 1:
                    pe.wait_ge(hg_k, level - 1)
                if level < LEVELS - 1:
                    for i in range(HG * NT):
                        hd, toks = i // NT, slice((i % NT) * P, (i % NT + 1) * P)
                        ins = mm(misc[:, i // 4, (i % 4) * P:(i % 4 + 1) * P], kr[:, hd, toks],
                                 qp[:, hd, toks], start=True, stop=True)
                else:
                    for hd in range(HG):
                        ins = mm(misc[:, hd // 4, (hd % 4) * P:(hd % 4 + 1) * P], kr[:, hd, 0:P],
                                 qp[:, hd, P:T], start=True, stop=True)
                ins.then_inc(hg_s, 1)

            def hg_output():
                pe.wait_ge(hg_acc, 2 * (LEVELS - 2))
                pe.wait_ge(hg_m, 2 * LEVELS)
                for hd in range(HG):
                    cols = slice(hd * P, (hd + 1) * P)
                    o = (hd % 2) * T
                    mm(misc[:, hd // 2, o:o + P], v_hg[:, 0, cols], acc[:, NT * hd, :],
                       start=True, stop=True)
                    mm(misc[:, hd // 2, o + P:o + T], v_hg[:, 1, cols], acc[:, NT * hd + 1, :],
                       start=True, stop=False)
                    ins = mm(misc[:, hd // 2, o + P:o + T], v_hg[:, 0, cols], cross[:, hd, :],
                             start=False, stop=True)
                ins.then_inc(hg_o, 1)

            def hg_squares():
                pe.wait_ge(hg_os, 4)
                pe.wait_ge(hg_o2, 4)
                for i in range(4):
                    ins = mm(misc[:, i, :], ones[:], o2_hg[:, 2 * i:2 * i + 2, :], start=True, stop=True)
                ins.then_inc(hg_ss, 1)

            def att_scores(u):
                if u == 0:
                    pe.wait_ge(hg_sd, 4)
                else:
                    pe.wait_ge(at_nm, u)
                f = slice(DH * (u % 2), DH * (u % 2) + DH)
                mm(ps[:, 4, 0:P], aq[f, u // 2, 0:P], ak[f, u // 2, 0:P], start=True, stop=True)
                mm(ps[:, 4, P:3 * P], aq[f, u // 2, P:T], ak[f, u // 2, :],
                   start=True, stop=True).then_inc(at_s, 1)

            def att_turn(u):
                pe.wait_ge(at_p, 2 * (u + 1))
                if u >= 1:
                    pe.wait_ge(at_pt, u)
                for i in range(3):
                    ins = nc.tensor.transpose(ps[:, 5, i * P:(i + 1) * P],
                                              prob[:, u % 3, i * P:(i + 1) * P], ident[:])
                ins.then_inc(at_t, 1)

            def att_values(u):
                pe.wait_ge(at_pt, u + 1)
                if u >= 4 and u % 2 == 0:
                    pe.wait_ge(at_y, u // 2 - 1)
                o = ps[DH * (u % 2):DH * (u % 2) + DH, 6 + (u // 2) % 2, :]
                cols = slice(u * DH, (u + 1) * DH)
                mm(o[:, 0:T], av[:, 0, cols], prob_t[:, u % 2, 0:T], start=True, stop=True)
                mm(o[:, P:T], av[:, 1, cols], prob_t[:, u % 2, T:T + P],
                   start=False, stop=True, skip_group_check=True).then_inc(at_pv, 1)

            for g in range(G_IN):
                c0, s = C_IN + NC * g, g % 2
                if g >= 2:
                    pe.wait_ge(set_free[s], g // 2)
                if g == 1:
                    pe.wait_ge(meta_ready, 1)
                natural = g in (4, 5, 12, 13)
                for k in range(NC):
                    if g == 0:
                        pe.wait_ge(x_ready, CK * (k + 1))
                    if natural:
                        chunk_n(c0, k, CK * k, xhi, xlo, s, k == 0, k == NC - 1)
                    else:
                        chunk_t(c0, k, CK * k, xhi, xlo, blocks(s), T, k == 0, k == NC - 1)
                    if k == 5 and g == 0:
                        turn_meta()
                    if k == 1 and G_LEVEL <= g < G_HGOUT:
                        level_scores(g - G_LEVEL)
                    if k == 1 and g == G_HGOUT:
                        hg_output()
                    if k == 6 and g == G_HGOUT:
                        hg_squares()
                    slot, odd = divmod(NC * (g - G_ATT) + k, 2)
                    if g >= G_ATT and not odd and slot < AH + 3:
                        if slot >= 3:
                            att_values(slot - 3)
                        if 2 <= slot < AH + 2:
                            att_turn(slot - 2)
                        if slot < AH:
                            att_scores(slot)

            pe.wait_ge(ya_ready, 4)
            with pe.Fori(0, 4) as n:
                c0 = C_BR + NC * n
                for s, (yh, yl) in enumerate(((ya_hi, ya_lo), (yb_hi, yb_lo))):
                    pe.wait_ge(set_free[s], G_IN // 2 + n)
                    if s == 1:
                        pe.wait_ge(at_y, AH // 2)
                    for k in range(NC // 2):
                        chunk_t(c0, NC // 2 * s + k, CK * k, yh, yl, blocks(s), T, k == 0, k == NC // 2 - 1)

            with pe.Fori(0, 2) as i:
                for s in range(2):
                    pe.wait_ge(set_free[s], G_IN // 2 + 4 + i)
                    for k in range(NC):
                        pe.wait_ge(br_ready, k // 2 + 1)
                        chunk_n(C_OUT + 2 * NC * i + NC * s, k, CK * k, xhi, xlo, s, k == 0, k == NC - 1)

            turn_normed(1)

            def quarter(q):
                c0 = C_FF + 8 * NC * q
                for g in range(4):
                    pe.wait_ge(set_free[g % 2], G_IN // 2 + 6 + 4 * q + g // 2)
                    for k in range(NC):
                        if g == 0:
                            pe.wait_ge(x_ready, KT + CK * (k + 1))
                        chunk_t(c0 + NC * g, k, CK * k, xhi, xlo, blocks(g % 2), T, k == 0, k == NC - 1)
                for g in range(4):
                    pe.wait_ge(set_free[g % 2], G_IN // 2 + 8 + 4 * q + g // 2)
                    for k in range(NC):
                        pe.wait_ge(up_ready, 4 * q + k // 2 + 1)
                        uh, ul = (ya_hi, ya_lo) if k < NC // 2 else (yb_hi, yb_lo)
                        chunk_n(c0 + 4 * NC + NC * g, k, CK * (k % (NC // 2)), uh, ul, g % 2, k == 0, k == NC - 1)

            with pe.Fori(0, QUARTERS - 1) as q:
                quarter(q)
            quarter(QUARTERS - 1)

            turn_normed(2)

            def values_turn(b):
                if b < 4:
                    pe.wait_ge(kvb_free, 2)
                else:
                    pe.wait_ge(vt_c[b % 2], (b - 4) // 2 + 1)
                o = ps[:, 4 + b % 4, :]
                nc.tensor.transpose(o[:, 0:P], v_t[:, b, 0:P], ident[:])
                nc.tensor.transpose(o[:, P:T], v_t[:, b, P:T], ident[:])
                nc.tensor.transpose(o[0:META, T:T + P], v_t[:, b, T:TM], ident[:]).then_inc(vt_t[b % 2], 1)

            def rope_squares(n, s):
                pe.wait_ge(nr_ev, 2 * n + 1)
                if n == 0:
                    pe.wait_ge(set_free[0], SETS_BEFORE_2 + 3)
                    pe.wait_ge(set_free[1], SETS_BEFORE_2 + 3)
                for i in range(2):
                    src = qsq[:, i, :] if n == 0 else qsq[:, 2 * i:2 * i + 2, 0:T]
                    w = TM if n == 0 else 2 * T
                    ins = mm(ps[:, 2 * s + i, 0:w], ones[:], src, start=True, stop=True)
                ins.then_inc(nr_ss, 1)

            def rope_turn_halves(n, s):
                pe.wait_ge(nr_sd, n + 1)
                for i in range(2):
                    src = qg[:, i, :] if n == 0 else qg[:, 2 * i:2 * i + 2, 0:T]
                    w = TM if n == 0 else 2 * T
                    ins = mm(ps[:, 2 * s + i, 0:w], turn[:], src, start=True, stop=True)
                ins.then_inc(nr_rot, 1)

            def b_scores(u):
                hd, t = divmod(u, NT)
                if hd in (0, H2 // 2) and t == 0:
                    s = 0 if hd == 0 else 1
                    pe.wait_ge(set_free[s], need2[5 + s] + 1)
                if u == 0:
                    for i in range(2):
                        pe.wait_ge(vt_c[i], 5)
                else:
                    pe.wait_ge(b_nm, u)
                for i in range(2):
                    f = slice(DH * i, DH * i + DH)
                    ins = mm(ps[:, 4 + i, 0:TM], qb[f, hd, t * P:(t + 1) * P], kb[f, hd, :], start=True, stop=True)
                ins.then_inc(b_s, 1)

            def p_turn(p, dst):
                nc.tensor.transpose(dst[:, 0:P], p[:, 0:P], ident[:])
                nc.tensor.transpose(dst[:, P:T], p[:, P:T], ident[:])
                return nc.tensor.transpose(dst[0:META, T:T + P], p[:, T:TM], ident[:])

            def pv(dst, vh, buf):
                mm(dst, v_nat[:, vh, 0, :], pt2[:, buf, 0:P], start=True, stop=False)
                mm(dst, v_nat[:, vh, 1, :], pt2[:, buf, P:T], start=False, stop=False)
                return mm(dst, v_meta[:, vh, :], pt2[0:META, buf, T:T + P], start=False, stop=True)

            def b_turn(u):
                pe.wait_ge(b_p, u + 1)
                if u >= 1:
                    pe.wait_ge(b_pt, 2 * u)
                p_turn(p2[:, u % 3, 0, :], ps[:, 6, :]).then_inc(b_t, 1)

            def b_values(u):
                pe.wait_ge(b_pt, 2 * (u + 1))
                if u >= 1:
                    pe.wait_ge(b_o, u)
                pv(ps[:, 7, 0:P], u // NT, u % 2).then_inc(b_pv, 1)

            def a_scores(v):
                hd, t = divmod(v, NT)
                if v == 0:
                    pe.wait_ge(nr_done, 3)
                    pe.wait_ge(b_nm, B_UNITS)
                else:
                    pe.wait_ge(a_exp, v)
                mm(ps[:, 4, 0:TM], qa[:, hd, t * P:(t + 1) * P], ka[:, hd // (H2 // KV2), :],
                   start=True, stop=True).then_inc(a_s, 1)

            def a_turn(v):
                pe.wait_ge(a_p, v + 1)
                if v >= 1:
                    pe.wait_ge(a_pt, 2 * v)
                else:
                    pe.wait_ge(b_pt, 2 * B_UNITS)
                p_turn(p2[:, v % 4 // 2, v % 2, :], ps[:, 6, :]).then_inc(a_t, 1)

            def a_values(v):
                pe.wait_ge(a_pt, 2 * (v + 1))
                if v >= 1:
                    pe.wait_ge(a_o, v)
                else:
                    pe.wait_ge(b_o, B_UNITS)
                pv(ps[:, 7, 0:P], 8 + v // NT // (H2 // KV2), v % 2).then_inc(a_pv, 1)

            def b_norm_squares(i):
                if i == 0:
                    pe.wait_ge(bn_o2, 1)
                    pe.wait_ge(b_nm, B_UNITS)
                else:
                    pe.wait_ge(bn_c, i)
                mm(ps[:, 5, :], ones[:], ob2[:, 2 * i:2 * i + 2, :], start=True, stop=True).then_inc(bn_ss, 1)

            def side(pos):
                slot, odd = divmod(pos, 2)
                if not odd and 0 <= slot < B_SLOTS:
                    if slot >= 3:
                        b_values(slot - 3)
                    if 2 <= slot < B_UNITS + 2:
                        b_turn(slot - 2)
                    if slot < B_UNITS:
                        b_scores(slot)
                v = pos - POS_A
                if 0 <= v < A_SLOTS:
                    if v >= 4:
                        a_values(v - 4)
                    if 3 <= v < A_UNITS + 3:
                        a_turn(v - 3)
                    if v < A_UNITS:
                        a_scores(v)
                if 0 <= pos - POS_BN < 8 and (pos - POS_BN) % 2 == 0:
                    b_norm_squares((pos - POS_BN) // 2)

            pe.wait_ge(c_in, 16 * N_CONST)
            for j in range(G_IN2):
                c0 = C_IN2 + NC * j
                kv = j < 5
                if kv and j % 2 == 0:
                    for s in range(2):
                        pe.wait_ge(set_free[s], SETS_BEFORE_2 + j // 2)
                    outs = [ps[:, b, 0:TM] for b in range(4)]
                elif kv:
                    if j == 3:
                        pe.wait_ge(kvb_free, 1)
                    outs = [ps[:, 4 + b, 0:TM] for b in range(4)]
                else:
                    s = (j - 5) % 2
                    pe.wait_ge(set_free[s], need2[j])
                    outs = blocks(s)
                for k in range(NC):
                    if j == 0:
                        pe.wait_ge(x_ready, 2 * KT + CK * (k + 1))
                    chunk_t(c0, k, CK * k, xhi, xlo, outs, TM if kv else T, k == 0, k == NC - 1, shared=not kv)
                    if j == 5 and 1 <= k <= 5:
                        values_turn(2 * (k - 1))
                        values_turn(2 * (k - 1) + 1)
                    for n, jn in enumerate((5, 8, 9)):
                        if j == jn and k == 1:
                            rope_squares(n, (1, 0, 1)[n])
                        if j == jn and k == 4:
                            rope_turn_halves(n, (1, 0, 1)[n])
                    if j >= J_B:
                        side(NC * (j - J_B) + k)
            for pos in range(NC * (G_IN2 - J_B), POS_A + A_SLOTS):
                side(pos)

            with pe.Fori(0, 2) as i:
                for s in range(2):
                    pe.wait_ge(set_free[s], sets_before_out2[s] + i)
                    for k in range(NC):
                        kt = CK * ((k + NC // 2) % NC)
                        if k < NC // 2:
                            pe.wait_ge(yb2_ready, 1)
                        else:
                            pe.wait_ge(ya2_ready, 1)
                        chunk_n(C_OUT2 + 2 * NC * i + NC * s, k, kt, xhi, xlo, s, k == 0, k == NC - 1)

        @block.scalar
        def _(act):
            f = nc.scalar.activation

            def split_hi(c0, k):
                act.wait_ge(raw_in[k % SLOTS], 4 * c0 + 16 * (k // SLOTS + 1))
                if not isinstance(c0, int) or c0 + k >= SLOTS:
                    act.wait_ge(pe_done, c0 + k - SLOTS + 1)
                f(whi[:, k % SLOTS], raw[:, k % SLOTS], ACT.Copy).then_inc(whi_ready, 1)

            def square(part, n, src, junk_, t, done):
                f(junk_, src, ACT.Square, accum_out=sq[:, part, t, n:n + 1]).then_inc(done, 1)

            def norm(b, src, w, col):
                act.wait_ge(n_sum, b + 1)
                f(ss[:, col:col + 2], ss[:, col:col + 2], ACT.Sqrt, bias=eps_t[:], scale=1.0 / D).then_inc(n_sd, 1)
                act.wait_ge(n_rs, b + 1)
                for i in range(4):
                    cols = slice(i * CW, (i + 1) * CW)
                    f(normed[:, 1, cols], src[:, 1, cols], ACT.Copy, scale=rstd[:, col + 1:col + 2]).then_inc(n_un1, 1)
                for kt in range(KT):
                    act.wait_ge(n_tr, KT // 2 * b + kt // 2 + 1)
                    f(xhi[:, kt, 0:T], ps[:, 4 + (kt % 8) // 2, (kt % 2) * T:(kt % 2) * T + T], ACT.Copy,
                      scale=w[:, kt:kt + 1]).then_inc(n_hi, 1)

            for t in range(NT):
                act.wait_ge(x_in[t], 16)
                for i in range(4):
                    cols = slice(i * CW, (i + 1) * CW)
                    square(0, i, x_nat[:, t, cols], junk[:, cols] if t == 0 else junk_b[:, cols], t, n_ss)
            act.wait_ge(setup, 1)
            act.wait_ge(mixw_in, 16)
            norm(0, x_nat, mix_w, 0)
            for k in range(LEAD):
                split_hi(C_IN, k)

            def start_meta():
                act.wait_ge(meta_in, 16)
                act.wait_ge(n_hi, KT)
                f(junk[0:META, :], meta_nat[:], ACT.Square, accum_out=ss[0:META, 8:9]).then_inc(m_ss, 1)
                act.wait_ge(m_ss, 1)
                f(ss[0:META, 8:9], ss[0:META, 8:9], ACT.Sqrt, bias=eps_t[0:META], scale=1.0 / D).then_inc(m_sd, 1)
                act.wait_ge(lb_max, 1)
                f(lbe[:], lbt[:], ACT.Exp).then_inc(lb_exp, 1)
                act.wait_ge(lam_sum, 1)
                f(lams[:, 2:4], lams[:, 0:2], ACT.Exp).then_inc(lam_exp, 1)

            def sigmoid(dst, s, done):
                f(dst, pset(s), ACT.Sigmoid).then_inc(done, 1)

            def evac_in(g):
                act.wait_ge(pe_done, C_IN + NC * (g + 1))
                s, half = g % 2, slice(4 * (g % 2), 4 * (g % 2) + 4)
                if g < 2:
                    sigmoid(qp[:, half, :], s, e_sig)
                elif g < 4:
                    sigmoid(g_even[:].rearrange("p (n t) -> p n t", t=T)[:, half, :], s, e_sig)
                elif g < 6:
                    f(v_hg[:, :, (g % 2) * CW:(g % 2 + 1) * CW], ps[:, 2 * s:2 * s + 2, :],
                      ACT.Copy).then_inc(set_free[s], 1)
                elif g < 8:
                    sigmoid(sg[:, half, :], s, e_sig)
                elif g < 10:
                    f(aq[:, half, :], pset(s), ACT.Copy, scale=DH ** -0.5).then_inc(set_free[s], 1)
                elif g < 12:
                    f(ak[:, half, :], pset(s), ACT.Copy).then_inc(set_free[s], 1)
                elif g < 14:
                    f(av[:, :, (g % 2) * CW:(g % 2 + 1) * CW], ps[:, 2 * s:2 * s + 2, :],
                      ACT.Copy).then_inc(set_free[s], 1)
                else:
                    sigmoid(gates[:, 4 * (g - 14):4 * (g - 14) + 4, :], s, set_free[s])

            def hg_copy(i):
                act.wait_ge(hg_o, 1)
                f(o_hg[:, 2 * i:2 * i + 2, :], misc[:, i, :].rearrange("p (x c) -> p x c", x=2),
                  ACT.Copy).then_inc(hg_os, 1)

            def hg_root(i):
                act.wait_ge(hg_ss, 1)
                f(rs_hg[:, 2 * i:2 * i + 2, :], misc[:, i, :].rearrange("p (x c) -> p x c", x=2), ACT.Sqrt,
                  bias=eps_t[:], scale=1.0 / P).then_inc(hg_sd, 1)

            def hg_upper(i):
                act.wait_ge(hg_y, i + 1)
                f(ya_hi[:, 2 * i:2 * i + 2, :], o_hg[:, 2 * i:2 * i + 2, :], ACT.Copy).then_inc(hg_hi, 1)

            def att_exp(u):
                act.wait_ge(at_nm, u + 1)
                for t, cols in enumerate((slice(0, P), slice(P, 3 * P))):
                    f(prob[:, u % 3, cols], prob[:, u % 3, cols], ACT.Exp, bias=nm[:, u % 3, t:t + 1],
                      scale=-1.0, accum_out=rsum[:, u % 3, t:t + 1]).then_inc(at_exp, 1)

            def att_copy(u):
                act.wait_ge(at_t, u + 1)
                if u >= 2:
                    act.wait_ge(at_pv, u - 1)
                f(prob_t[:, u % 2, :], ps[:, 5, 0:3 * P], ACT.Copy).then_inc(at_pt, 1)

            def att_upper(j):
                act.wait_ge(at_pv, 2 * (j + 1))
                f(yb_hi[:, j, :], ps[:, 6 + j % 2, 0:T], ACT.Copy).then_inc(at_hi, 1)

            for g in range(G_IN):
                for k in range(NC):
                    split_hi(C_IN + NC * g, LEAD + k)
                    if g == 0 and k == 2:
                        start_meta()
                    if g == 0 and k == 6:
                        act.wait_ge(m_w, 1)
                        f(xhi[:, :, T:TM], meta_t[:], ACT.Copy).then_inc(m_hi, 1)
                    if g == G_HGOUT and 2 <= k <= 5:
                        hg_copy(k - 2)
                    if g == G_HGOUT and k == 7:
                        for i in range(4):
                            hg_root(i)
                    if g == G_HGOUT + 3 and k % 2 == 0:
                        hg_upper(k // 2)
                    slot, odd = divmod(NC * (g - G_ATT) + k, 2)
                    if g >= G_ATT and odd and slot < AH + 3:
                        if 2 <= slot < AH + 2:
                            att_copy(slot - 2)
                        if slot < AH:
                            att_exp(slot)
                        if slot >= 4 and slot % 2 == 0:
                            att_upper((slot - 4) // 2)
                evac_in(g)

            with act.Fori(0, 4) as n:
                for k in range(NC):
                    split_hi(C_BR + NC * n, LEAD + k)
                act.wait_ge(br_m, n + 1)
                f(xhi[:, bass.ds(4 * n, 4), 0:T], both[:], ACT.Copy).then_inc(br_hi, 1)
            def h_squares(part, n, free, done):
                act.wait_ge(set_free[n % 2], free)
                for t in range(NT):
                    cols = slice(n * CW, (n + 1) * CW)
                    square(part, n, h[:, t, cols], (junk, junk_b)[t][:, cols], t, done)

            for n in range(4):
                for k in range(NC):
                    split_hi(C_OUT + NC * n, LEAD + k)
                h_squares(1, n, G_IN // 2 + 4 + n // 2 + 1, n_ss)
            norm(1, h, mlp_w, 2)

            def quarter(q, last):
                c0 = C_FF + 8 * NC * q
                for g in range(4):
                    for k in range(NC):
                        split_hi(c0 + NC * g, LEAD + k)
                    act.wait_ge(pe_done, c0 + NC * (g + 1))
                    f(relu[:], pset(g % 2), ACT.Relu).then_inc(set_free[g % 2], 1)
                    act.wait_ge(up_sq, 4 * q + g + 1)
                    dst = (ya_hi, yb_hi)[g // 2]
                    f(dst[:, 4 * (g % 2):4 * (g % 2) + 4, :], relu2[:], ACT.Copy).then_inc(up_hi, 1)
                for g in range(4):
                    for k in range(NC):
                        split_hi(c0 + 4 * NC + NC * g, LEAD + k)
                    if last:
                        h_squares(1, g, G_IN // 2 + 8 + 4 * q + g // 2 + 1, f_sq)
                        act.wait_ge(f_w, g + 1)
                        for t in range(NT):
                            cols = slice(g * CW, (g + 1) * CW)
                            square(2, g, h[:, t, cols], (junk3, junk3_b)[t][:, cols], t, n_ss)

            with act.Fori(0, QUARTERS - 1) as q:
                quarter(q, False)
            quarter(QUARTERS - 1, True)
            act.wait_ge(f_un, 1)
            f(ss[:, 4:6], ss[:, 4:6], ACT.Sqrt, bias=eps_t[:], scale=1.0 / D).then_inc(f_un, 1)
            norm(2, h, pre_w, 6)

            def evac_in2(j):
                act.wait_ge(pe_done, C_IN2 + NC * (j + 1))
                if j in (0, 2):
                    for s in range(2):
                        dst = kb if j == 0 else v_t
                        f(dst[:, (0 if j == 0 else 0) + 2 * s:2 * s + 2, :], ps[:, 2 * s:2 * s + 2, 0:TM],
                          ACT.Copy).then_inc(set_free[s], 1)
                elif j in (1, 3):
                    dst = kb if j == 1 else v_t
                    f(dst[:, 4:8, :], ps[:, 4:8, 0:TM], ACT.Copy).then_inc(kvb_free, 1)
                elif j == 4:
                    f(qg[:, 0:2, :], ps[:, 0:2, 0:TM], ACT.Copy, scale=gvec[:, 2:3]).then_inc(nr_ev, 1)
                    f(qsq[:, 0:2, :], ps[:, 0:2, 0:TM], ACT.Square).then_inc(set_free[0], 1)
                    f(v_t[:, 8:10, :], ps[:, 2:4, 0:TM], ACT.Copy).then_inc(set_free[1], 1)
                elif j in (5, 6):
                    s = (j - 5) % 2
                    f(qb[:, 4 * s:4 * s + 4, :], pset(s), ACT.Copy, scale=DH ** -0.5).then_inc(set_free[s], 1)
                elif j in (7, 8):
                    n = j - 6
                    act.wait_ge(nr_done, n)
                    f(qg[:, :, 0:T], pset(n - 1), ACT.Copy, scale=gvec[:, 1:2]).then_inc(nr_ev, 1)
                    f(qsq[:, :, 0:T], pset(n - 1), ACT.Square).then_inc(nr_ev, 1)
                else:
                    g = (j - 9)
                    dst = gb if g < 2 else ga
                    sigmoid(dst[:, 4 * (g % 2):4 * (g % 2) + 4, :], g % 2, e_sig)

            def values_copy(b):
                act.wait_ge(vt_t[1], b // 2 + 1)
                f(v_nat[:, b, :, :], ps[:, 4 + b % 4, 0:T].rearrange("p (t c) -> p t c", t=2), ACT.Copy)
                f(v_meta[:, b, :], ps[0:META, 4 + b % 4, T:T + P], ACT.Copy).then_inc(vt_c[1], 1)

            def rope_root(n, s):
                act.wait_ge(nr_ss, n + 1)
                if n == 0:
                    dst, src = qsq[:, 0:2, :], ps[:, 2 * s:2 * s + 2, 0:TM]
                else:
                    dst, src = qsq[:, :, 0:T], pset(s)
                f(dst, src, ACT.Sqrt, bias=eps_t[:], scale=1.0 / P).then_inc(nr_sd, 1)

            def b_exp_(u):
                act.wait_ge(b_nm, u + 1)
                for i in range(2):
                    f(p2[:, u % 3, i, :], p2[:, u % 3, i, :], ACT.Exp, bias=nm[:, u % 3, i:i + 1], scale=-1.0,
                      accum_out=rsum[:, u % 3, i:i + 1]).then_inc(b_exp, 1)

            def p_copy(buf, done):
                f(pt2[:, buf, 0:T], ps[:, 6, 0:T], ACT.Copy).then_inc(done, 1)
                f(pt2[0:META, buf, T:T + P], ps[0:META, 6, T:T + P], ACT.Copy).then_inc(done, 1)

            def b_copy(u):
                act.wait_ge(b_t, u + 1)
                if u >= 2:
                    act.wait_ge(b_pv, u - 1)
                p_copy(u % 2, b_pt)

            def b_out(u):
                act.wait_ge(b_pv, u + 1)
                f(ob[:, u // NT, (u % NT) * P:(u % NT + 1) * P], ps[:, 7, 0:P], ACT.Copy).then_inc(b_o, 1)

            def a_exp_(v):
                act.wait_ge(a_nm, v + 1)
                f(p2[:, v % 4 // 2, v % 2, :], ps[:, 4, 0:TM], ACT.Exp, bias=nm[:, v % 4, 0:1], scale=P ** -0.5,
                  accum_out=rsum[:, v % 4, 0:1]).then_inc(a_exp, 1)

            def a_copy(v):
                act.wait_ge(a_t, v + 1)
                if v >= 2:
                    act.wait_ge(a_pv, v - 1)
                else:
                    act.wait_ge(b_pv, B_UNITS)
                p_copy(v % 2, a_pt)

            def side(pos):
                slot, odd = divmod(pos, 2)
                if odd and 0 <= slot < B_SLOTS:
                    if 2 <= slot < B_UNITS + 2:
                        b_copy(slot - 2)
                    if slot < B_UNITS:
                        b_exp_(slot)
                    if slot >= 3:
                        b_out(slot - 3)
                v = pos - POS_A
                if 0 <= v < A_SLOTS:
                    if 3 <= v < A_UNITS + 3:
                        a_copy(v - 3)
                    if v < A_UNITS:
                        a_exp_(v)
                i = (pos - POS_BN) // 2
                if 0 <= pos - POS_BN < 8 and (pos - POS_BN) % 2 == 0:
                    act.wait_ge(bn_ss, i + 1)
                    f(obr[:, 2 * i:2 * i + 2, :], ps[:, 5, :].rearrange("p (x c) -> p x c", x=2),
                      ACT.Copy).then_inc(bn_c, 1)
                if pos == POS_BN + 7:
                    act.wait_ge(bn_c, 4)
                    f(obr[:], obr[:], ACT.Sqrt, bias=eps_t[:], scale=1.0 / P).then_inc(bn_sd, 1)

            for j in range(G_IN2):
                for k in range(NC):
                    split_hi(C_IN2 + NC * j, LEAD + k)
                    if j == 5 and 2 <= k <= 6:
                        values_copy(2 * (k - 2) + 1)
                    for n, jn in enumerate((5, 8, 9)):
                        if j == jn and k == 2:
                            rope_root(n, (1, 0, 1)[n])
                    if j >= J_B:
                        side(NC * (j - J_B) + k)
                evac_in2(j)
            for pos in range(NC * (G_IN2 - J_B), POS_A + A_SLOTS):
                side(pos)
            act.wait_ge(bn_y, 1)
            act.wait_ge(pe_done, C_OUT2)
            f(xhi[:, 8:16, 0:T], ob[:], ACT.Copy).then_inc(bn_hi, 1)
            act.wait_ge(an_y, 1)
            f(xhi[:, 0:8, 0:T], oa[:], ACT.Copy).then_inc(an_hi, 1)
            for g in range(4):
                for k in range(NC):
                    if NC * g + LEAD + k < 4 * NC:
                        split_hi(C_OUT2 + NC * g, LEAD + k)
                act.wait_ge(pe_done, C_OUT2 + NC * (g + 1))
                f(y2[:, :, g * CW:(g + 1) * CW], ps[:, 2 * (g % 2):2 * (g % 2) + 2, :],
                  ACT.Copy).then_inc(set_free[g % 2], 1)
            for s in range(2):
                act.wait_ge(set_free[s], sets_before_out2[s] + 2)
            for t in range(NT):
                f(junk2[:], y2[:, t], ACT.Square, accum_out=ss[:, 10 + t:11 + t]).then_inc(y_ss, 1)
                act.wait_ge(y_ss, t + 1)
            f(ss[:, 10:12], ss[:, 10:12], ACT.Sqrt, bias=eps_t[:], scale=1.0 / D).then_inc(y_sd, 1)

        @block.vector
        def _(dve):
            tt, ts, stt = nc.vector.tensor_tensor, nc.vector.tensor_scalar, nc.vector.scalar_tensor_tensor
            steps = [0]

            def own(ins):
                steps[0] += 1
                ins.then_inc(dve_step, 1)
                dve.wait_ge(dve_step, steps[0])

            def split_lo(c0, k):
                dve.wait_ge(whi_ready, c0 + k + 1)
                tt(wlo[:, k % SLOTS], raw[:, k % SLOTS], whi[:, k % SLOTS], ALU.subtract).then_inc(wlo_ready, 1)

            def norm(b, src, w, col):
                dve.wait_ge(n_sd, b + 1)
                nc.vector.reciprocal(rstd[:, col:col + 2], ss[:, col:col + 2]).then_inc(n_rs, 1)
                norm_tail(b, src, w, col)

            def norm_tail(b, src, w, col):
                dve.wait_ge(n_rs, b + 1)
                for i in range(4):
                    cols = slice(i * CW, (i + 1) * CW)
                    ts(normed[:, 0, cols], src[:, 0, cols], rstd[:, col:col + 1], None, ALU.mult).then_inc(n_un0, 1)
                for kt in range(KT):
                    dve.wait_ge(n_hi, KT * b + kt // 2 * 2 + 2)
                    stt(out=xlo[:, kt, 0:T], in0=ps[:, 4 + (kt % 8) // 2, (kt % 2) * T:(kt % 2) * T + T],
                        scalar=w[:, kt:kt + 1], in1=xhi[:, kt, 0:T], op0=ALU.mult,
                        op1=ALU.subtract).then_inc(x_ready, 1)

            nc.vector.memset(eps_t[:], EPS).then_inc(setup, 1)
            own(nc.vector.memset(ones[:], 1.0))
            dve.wait_ge(n_ss, 8)
            nc.vector.tensor_reduce(ss[:, 0:2], sq[:, 0], AX.X, ALU.add).then_inc(n_sum, 1)
            norm(0, x_nat, mix_w, 0)
            for k in range(LEAD):
                split_lo(C_IN, k)

            def start_small():
                dve.wait_ge(c_in, 16 * N_CONST)
                own(tt(lbs[:, 0], lbt[:, 0], lbt[:, 1], ALU.max))
                own(tt(lbt[:, 0], lbt[:, 0], lbs[:, 0], ALU.subtract))
                tt(lbt[:, 1], lbt[:, 1], lbs[:, 0], ALU.subtract).then_inc(lb_max, 1)
                own(tt(lamv[:, 0], lamv[:, 0], lamv[:, 1], ALU.mult))
                own(tt(lamv[:, 2], lamv[:, 2], lamv[:, 3], ALU.mult))
                nc.vector.tensor_reduce(lams[:, 0:2], lamv[:, 0:4:2, :], AX.X, ALU.add).then_inc(lam_sum, 1)
                own(ts(subg[:], gvec[:, 3:4], 1.0 - LAMBDA_INIT, None, ALU.mult))

            def start_meta():
                dve.wait_ge(m_sd, 1)
                own(nc.vector.reciprocal(rstd[0:META, 8:9], ss[0:META, 8:9]))
                ts(meta_nat[:], meta_nat[:], rstd[0:META, 8:9], None, ALU.mult).then_inc(m_un, 1)
                dve.wait_ge(lb_exp, 1)
                own(tt(lbs[:, 1], lbe[:, 0], lbe[:, 1], ALU.add))
                own(nc.vector.reciprocal(lbs[:, 1], lbs[:, 1]))
                own(tt(lbs[:, 2], lbe[:, 0], lbs[:, 1], ALU.mult))
                own(ts(lbs[:, 3], lbs[:, 2], -1.0, 1.0, ALU.mult, ALU.add))
                dve.wait_ge(lam_exp, 1)
                own(tt(lams[:, 4:5], lams[:, 3:4], lams[:, 2:3], ALU.subtract))
                own(ts(lams[:, 5:6], lams[:, 4:5], -LAMBDA_INIT, None, ALU.add))

            def meta_weights():
                dve.wait_ge(m_tr, 1)
                tt(meta_t[:], ps[:, 3, 0:KT * META].rearrange("p (k m) -> p k m", k=KT),
                   spread(pre_w[:], [1, KT], [0, META]), ALU.mult).then_inc(m_w, 1)

            def meta_lower():
                dve.wait_ge(m_hi, 1)
                tt(xlo[:, :, T:TM], meta_t[:], xhi[:, :, T:TM], ALU.subtract).then_inc(meta_ready, 1)

            def evac_in(g):
                s, half = g % 2, slice(4 * (g % 2), 4 * (g % 2) + 4)
                if g not in E_STEP:
                    return
                dve.wait_ge(e_sig, E_STEP[g] + 1)
                if g < 2:
                    stt(out=qp[:, half, :], in0=pset(s), scalar=P ** -0.5, in1=qp[:, half, :], op0=ALU.mult,
                        op1=ALU.mult).then_inc(set_free[s], 1)
                elif g < 4:
                    gg = g_even[:].rearrange("p (n t) -> p n t", t=T)[:, half, :]
                    for b in range(4):
                        hd = 4 * s + b
                        ins = ts(gg[:, b, :], gg[:, b, :], lbs[:, 3, hd:hd + 1], lbs[:, 2, hd:hd + 1], ALU.mult, ALU.add)
                    own(ins)
                    ts(kr[:, half, :], gg, -1.0, 1.0, ALU.mult, ALU.add).then_inc(set_free[s], 1)
                else:
                    stt(out=sg[:, half, :], in0=pset(s), scalar=gvec[:, 0:1], in1=sg[:, half, :], op0=ALU.mult,
                        op1=ALU.mult).then_inc(set_free[s], 1)

            def level_mask(level, i):
                if i == 0:
                    dve.wait_ge(hg_s, level + 1)
                half = slice(8 * i, 8 * i + 8)
                if level == LEVELS - 1:
                    nc.vector.tensor_copy(cross[:, 4 * i:4 * i + 4, :],
                                          misc[:, i, :].rearrange("p (x c) -> p x c", x=4)).then_inc(hg_m, 1)
                    return
                src = misc[:, 2 * i:2 * i + 2, :].rearrange("p b (x c) -> p (b x) c", x=4)
                if level == 0 and i == 0:
                    dve.wait_ge(mask_in, 16)
                if level >= 2:
                    dve.wait_ge(hg_acc, 2 * (level - 2) + i + 1)
                dst = acc if level == 0 else masked
                tt(dst[:, half, :], src, spread(masks[:, level, :], [0, 8], [1, P]), ALU.mult).then_inc(hg_m, 1)

            def q_decay(level):
                flat = qp[:].rearrange("p n t -> p (n t)")
                if level == 0:
                    tt(flat, flat, g_even[:], ALU.mult).then_inc(hg_q, 1)
                    return
                hb = 2 ** (level - 1)
                n = HG * T // (2 * hb)
                src = (g_even, g_odd)[(level - 1) % 2]
                if level >= 2:
                    dve.wait_ge(hg_g, level - 1)
                v = flat.rearrange("p (n two h) -> p n two h", two=2, h=hb)[:, :, 1, :]
                tt(v, v, spread(src[:, 0:1], [2, n], [0, hb]), ALU.mult).then_inc(hg_q, 1)

            def hg_inverse(i):
                dve.wait_ge(hg_sd, i + 1)
                nc.vector.reciprocal(rs_hg[:, 2 * i:2 * i + 2, :], rs_hg[:, 2 * i:2 * i + 2, :]).then_inc(hg_rs, 1)

            def hg_scale(i):
                dve.wait_ge(hg_t, i // 2 + 1)
                dve.wait_ge(hg_rs, i + 1)
                tt(o_hg[:, 2 * i:2 * i + 2, :], o_hg[:, 2 * i:2 * i + 2, :], rs_hg[:, 2 * i:2 * i + 2, :],
                   ALU.mult).then_inc(hg_y, 1)

            def hg_lower(i):
                dve.wait_ge(hg_hi, i + 1)
                tt(ya_lo[:, 2 * i:2 * i + 2, :], o_hg[:, 2 * i:2 * i + 2, :], ya_hi[:, 2 * i:2 * i + 2, :],
                   ALU.subtract).then_inc(ya_ready, 1)

            def att_bias(u):
                dve.wait_ge(at_s, u + 1)
                if u % 2 == 0:
                    dve.wait_ge(rel_ready, u // 2 + 1)
                if u >= 3:
                    dve.wait_ge(at_t, u - 2)
                rb = rel[:, (u // 2) % 2, u % 2, :]
                stt(out=prob[:, u % 3, 0:P], in0=ps[:, 4, 0:P], scalar=-1.0, in1=rb[:, 0:P][:, ::-1], op0=ALU.mult,
                    op1=ALU.subtract)
                own(stt(out=prob[:, u % 3, P:3 * P], in0=ps[:, 4, P:3 * P], scalar=-1.0, in1=rb[:, ::-1], op0=ALU.mult,
                        op1=ALU.subtract))
                own(nc.vector.tensor_reduce(nm[:, u % 3, 0:1], prob[:, u % 3, 0:P], AX.X, ALU.min))
                nc.vector.tensor_reduce(nm[:, u % 3, 1:2], prob[:, u % 3, P:3 * P], AX.X, ALU.min).then_inc(at_nm, 1)

            def att_inverse(u):
                dve.wait_ge(at_exp, 2 * (u + 1))
                own(nc.vector.reciprocal(rinv[:, u % 3, :], rsum[:, u % 3, :]))
                for t, cols in enumerate((slice(0, P), slice(P, 3 * P))):
                    ts(prob[:, u % 3, cols], prob[:, u % 3, cols], rinv[:, u % 3, t:t + 1], None,
                       ALU.mult).then_inc(at_p, 1)

            def att_lower(j):
                dve.wait_ge(at_hi, j + 1)
                tt(yb_lo[:, j, :], ps[:, 6 + j % 2, 0:T], yb_hi[:, j, :], ALU.subtract).then_inc(at_y, 1)

            for g in range(G_IN):
                for k in range(NC):
                    split_lo(C_IN + NC * g, LEAD + k)
                    if G_LEVEL <= g < G_HGOUT:
                        level = g - G_LEVEL
                        if k in (2, 3):
                            level_mask(level, k - 2)
                        if k == 4 and level < LEVELS - 1:
                            q_decay(level)
                    if g == 0 and k in (1, 3, 5, 7):
                        (start_small, start_meta, meta_weights, meta_lower)[k // 2]()
                    if g == G_HGOUT + 1 and k % 2 == 0:
                        hg_inverse(k // 2)
                    if g == G_HGOUT + 2 and k % 2 == 1:
                        hg_scale(k // 2)
                    if g == G_HGOUT + 3 and k % 2 == 1:
                        hg_lower(k // 2)
                    slot, odd = divmod(NC * (g - G_ATT) + k, 2)
                    if g >= G_ATT and not odd:
                        if 1 <= slot < AH + 1:
                            att_inverse(slot - 1)
                        if slot < AH:
                            att_bias(slot)
                    if g >= G_ATT and odd and slot < AH + 3 and slot >= 4 and slot % 2 == 0:
                        att_lower((slot - 4) // 2)
                evac_in(g)

            with dve.Fori(0, 4) as n:
                c0 = C_BR + NC * n
                for k in range(4):
                    split_lo(c0, LEAD + k)
                dve.wait_ge(pe_done, c0 + 4)
                tt(part_a[:], pset(0), gates[:, bass.ds(4 * n, 4), :], ALU.mult).then_inc(set_free[0], 1)
                for k in range(4, 8):
                    split_lo(c0, LEAD + k)
                dve.wait_ge(pe_done, c0 + 8)
                tt(part_b[:], pset(1), gates[:, bass.ds(4 * n + 16, 4), :], ALU.mult).then_inc(set_free[1], 1)
                dve.wait_ge(br_hi, n + 1)
                tt(xlo[:, bass.ds(4 * n, 4), 0:T], both[:], xhi[:, bass.ds(4 * n, 4), 0:T],
                   ALU.subtract).then_inc(br_ready, 1)
            dve.wait_ge(h_in, 16)
            with dve.Fori(0, 2) as i:
                for s in range(2):
                    c0 = C_OUT + 2 * NC * i + NC * s
                    for k in range(NC):
                        split_lo(c0, LEAD + k)
                    dve.wait_ge(pe_done, c0 + NC)
                    hv = h[:, :, bass.ds(2 * CW * i + CW * s, CW)]
                    tt(hv, hv, ps[:, 2 * s:2 * s + 2, :], ALU.add).then_inc(set_free[s], 1)
            dve.wait_ge(n_ss, 16)
            nc.vector.tensor_reduce(ss[:, 2:4], sq[:, 1], AX.X, ALU.add).then_inc(n_sum, 1)
            norm(1, h, mlp_w, 2)

            def quarter(q, last):
                c0 = C_FF + 8 * NC * q
                for g in range(4):
                    for k in range(NC):
                        split_lo(c0 + NC * g, LEAD + k)
                    dve.wait_ge(up_hi, 4 * q + g + 1)
                    dh, dl = ((ya_hi, ya_lo), (yb_hi, yb_lo))[g // 2]
                    bs = slice(4 * (g % 2), 4 * (g % 2) + 4)
                    tt(dl[:, bs, :], relu2[:], dh[:, bs, :], ALU.subtract).then_inc(up_ready, 1)
                for g in range(4):
                    for k in range(NC):
                        split_lo(c0 + 4 * NC + NC * g, LEAD + k)
                    dve.wait_ge(pe_done, c0 + 4 * NC + NC * (g + 1))
                    hv = h[:, :, g * CW:(g + 1) * CW]
                    tt(hv, hv, ps[:, 2 * (g % 2):2 * (g % 2) + 2, :], ALU.add).then_inc(set_free[g % 2], 1)
                    if last:
                        if g == 0:
                            dve.wait_ge(finw_in, 16)
                        dve.wait_ge(f_sq, 2 * (g + 1))
                        tt(hv, hv, spread(fin_w[:, g * CW:(g + 1) * CW], [0, NT], [1, CW]), ALU.mult).then_inc(f_w, 1)

            with dve.Fori(0, QUARTERS - 1) as q:
                quarter(q, False)
            quarter(QUARTERS - 1, True)
            nc.vector.tensor_reduce(ss[:, 4:6], sq[:, 1], AX.X, ALU.add).then_inc(f_un, 1)
            dve.wait_ge(n_ss, 24)
            own(nc.vector.tensor_reduce(ss[:, 6:8], sq[:, 2], AX.X, ALU.add))
            dve.wait_ge(f_un, 2)
            own(nc.vector.reciprocal(rstd[:, 4:6], ss[:, 4:6]))
            own(tt(ss[:, 6:8], ss[:, 6:8], rstd[:, 4:6], ALU.mult))
            tt(ss[:, 6:8], ss[:, 6:8], rstd[:, 4:6], ALU.mult).then_inc(n_sum, 1)
            dve.wait_ge(n_sd, 3)
            own(nc.vector.reciprocal(rstd[:, 12:14], ss[:, 6:8]))
            tt(rstd[:, 6:8], rstd[:, 12:14], rstd[:, 4:6], ALU.mult).then_inc(n_rs, 1)
            norm_tail(2, h, pre_w, 6)

            def values_copy(b):
                dve.wait_ge(vt_t[0], b // 2 + 1)
                nc.vector.tensor_copy(v_nat[:, b, :, :], ps[:, 4 + b % 4, 0:T].rearrange("p (t c) -> p t c", t=2))
                nc.vector.tensor_copy(v_meta[:, b, :], ps[0:META, 4 + b % 4, T:T + P]).then_inc(vt_c[0], 1)

            def rope_inverse(n):
                dve.wait_ge(nr_sd, n + 1)
                v = qsq[:, 0:2, :] if n == 0 else qsq[:, :, 0:T]
                nc.vector.reciprocal(v, v).then_inc(nr_rs, 1)

            def rope_sin(n, s):
                dve.wait_ge(nr_rot, n + 1)
                if n == 0:
                    tt(qrot[:, 0:2, :], ps[:, 2 * s:2 * s + 2, 0:TM], spread(sin_t[:], [0, 2], [1, TM]),
                       ALU.mult).then_inc(set_free[s], 1)
                else:
                    tt(qrot[:, :, 0:T], pset(s), spread(sin_t[:], [0, 4], [1, T]), ALU.mult).then_inc(set_free[s], 1)

            def evac_in2(j):
                if j < 9:
                    return
                g = j - 9
                s, half = g % 2, slice(4 * (g % 2), 4 * (g % 2) + 4)
                dve.wait_ge(e_sig, N_E1 + g + 1)
                dst = (gb if g < 2 else ga)[:, half, :]
                stt(out=dst, in0=pset(s), scalar=subg[:] if g < 2 else 1.0, in1=dst, op0=ALU.mult,
                    op1=ALU.mult).then_inc(set_free[s], 1)

            def b_bias(u):
                hd, t = divmod(u, NT)
                dve.wait_ge(b_s, u + 1)
                if u >= 3:
                    dve.wait_ge(b_t, u - 2)
                own(stt(out=p2[:, u % 3, :, :], in0=spread(dist[:, t, :], [0, 2], [1, TM]),
                        scalar=float(2.0 ** (-8.0 * (hd + 1.0) / H2)), in1=ps[:, 4:6, 0:TM], op0=ALU.mult,
                        op1=ALU.subtract))
                nc.vector.tensor_reduce(nm[:, u % 3, :], p2[:, u % 3, :, :], AX.X, ALU.min).then_inc(b_nm, 1)

            def b_inverse(u):
                dve.wait_ge(b_exp, 2 * (u + 1))
                own(nc.vector.reciprocal(rinv[:, u % 3, :], rsum[:, u % 3, :]))
                own(ts(rinv[:, u % 3, 1:2], rinv[:, u % 3, 1:2], lams[:, 5:6], None, ALU.mult))

            def b_mix(u):
                own(ts(p2[:, u % 3, 0, :], p2[:, u % 3, 0, :], rinv[:, u % 3, 0:1], None, ALU.mult))
                stt(out=p2[:, u % 3, 0, :], in0=p2[:, u % 3, 1, :], scalar=rinv[:, u % 3, 1:2],
                    in1=p2[:, u % 3, 0, :], op0=ALU.mult, op1=ALU.add).then_inc(b_p, 1)

            def a_max(v):
                dve.wait_ge(a_s, v + 1)
                if v == 0:
                    dve.wait_ge(b_exp, 2 * B_UNITS)
                own(nc.vector.tensor_reduce(nm[:, v % 4, 1:2], ps[:, 4, 0:TM], AX.X, ALU.max))
                ts(nm[:, v % 4, 0:1], nm[:, v % 4, 1:2], -P ** -0.5, None, ALU.mult).then_inc(a_nm, 1)

            def a_inverse(v):
                dve.wait_ge(a_exp, v + 1)
                own(nc.vector.reciprocal(rinv[:, v % 4, 0:1], rsum[:, v % 4, 0:1]))
                ts(p2[:, v % 4 // 2, v % 2, :], p2[:, v % 4 // 2, v % 2, :], rinv[:, v % 4, 0:1], None,
                   ALU.mult).then_inc(a_p, 1)

            def a_out(v):
                dve.wait_ge(a_pv, v + 1)
                nc.vector.tensor_copy(oa[:, v // NT, (v % NT) * P:(v % NT + 1) * P], ps[:, 7, 0:P]).then_inc(a_o, 1)

            def side(pos):
                slot, odd = divmod(pos, 2)
                if not odd and 0 <= slot < B_SLOTS:
                    if 1 <= slot < B_UNITS + 1:
                        b_inverse(slot - 1)
                        b_mix(slot - 1)
                    if slot < B_UNITS:
                        b_bias(slot)
                v = pos - POS_A
                if 0 <= v < A_SLOTS:
                    if 1 <= v < A_UNITS + 1:
                        a_inverse(v - 1)
                    if v < A_UNITS:
                        a_max(v)
                    if v >= 4:
                        a_out(v - 4)
                if pos == POS_BN + 8:
                    dve.wait_ge(bn_sd, 1)
                    nc.vector.reciprocal(obr[:], obr[:]).then_inc(bn_rs, 1)

            for j in range(G_IN2):
                for k in range(NC):
                    split_lo(C_IN2 + NC * j, LEAD + k)
                    if j == 0 and k in (2, 4):
                        t = k // 2 - 1
                        dve.wait_ge(n_un1, 12)
                        ts(h[:, t], h[:, t], rstd[:, 4 + t:5 + t], None, ALU.mult).then_inc(h_ready, 1)
                    if j == 5 and 2 <= k <= 6:
                        values_copy(2 * (k - 2))
                    for n, jn in enumerate((5, 8, 9)):
                        if j == jn and k == 3:
                            rope_inverse(n)
                        if j == jn and k == 5:
                            rope_sin(n, (1, 0, 1)[n])
                    if j >= J_B:
                        side(NC * (j - J_B) + k)
                evac_in2(j)
            for pos in range(NC * (G_IN2 - J_B), POS_A + A_SLOTS):
                side(pos)
            dve.wait_ge(bn_hi, 1)
            tt(xlo[:, 8:16, 0:T], ob[:], xhi[:, 8:16, 0:T], ALU.subtract).then_inc(yb2_ready, 1)
            dve.wait_ge(an_hi, 1)
            tt(xlo[:, 0:8, 0:T], oa[:], xhi[:, 0:8, 0:T], ALU.subtract).then_inc(ya2_ready, 1)
            for c in range(LEAD, 4 * NC):
                split_lo(C_OUT2, c)
            dve.wait_ge(y_sd, 1)
            own(nc.vector.reciprocal(rstd[:, 10:12], ss[:, 10:12]))
            dve.wait_ge(postw_in, 16)
            dve.wait_ge(h_ready, NT)
            for t in range(NT):
                stt(out=y2[:, t], in0=y2[:, t], scalar=rstd[:, 10 + t:11 + t], in1=post_w[:], op0=ALU.mult,
                    op1=ALU.mult).then_inc(y_n, 1)
                dve.wait_ge(y_n, t + 1)
                tt(y2[:, t], y2[:, t], h[:, t], ALU.add).then_inc(y_out, 1)

        @block.gpsimd
        def _(pool):
            tt = nc.gpsimd.tensor_tensor

            def load(dst, src):
                return pool.dma_start(dst, src, allow_slow_non_contiguous=True)

            load(mix_w[:], norm_mix_w[0].rearrange("(k p) -> p k", p=P)).then_inc(mixw_in, 16)
            small = [
                (lbt[:, 0], lb_logits[0].rearrange("(k p) -> p k", p=P)),
                (lbt[:, 1], lb_logits[1].rearrange("(k p) -> p k", p=P)),
                (gvec[:, 0:1], hg_norm_w[0].rearrange("(p k) -> p k", k=1)),
                (gvec[:, 1:2], q_norm_g_2[0].rearrange("(p k) -> p k", k=1)),
                (gvec[:, 2:3], k_norm_g_2[0].rearrange("(p k) -> p k", k=1)),
                (gvec[:, 3:4], subln_g_2[0].rearrange("(p k) -> p k", k=1)),
                (lamv[:, 0], row_all(lambda_q1_2, DH)), (lamv[:, 1], row_all(lambda_k1_2, DH)),
                (lamv[:, 2], row_all(lambda_q2_2, DH)), (lamv[:, 3], row_all(lambda_k2_2, DH)),
                (mlp_w[:], norm_mlp_w[0].rearrange("(k p) -> p k", p=P)),
                (pre_w[:], pre_norm_g_2[0].rearrange("(k p) -> p k", p=P)),
                (cos_t[:], rope_cos), (sin_t[:], rope_sin), (turn[:], rope_turn),
                (dist[:], distance.rearrange("(t p) k -> p t k", p=P)),
            ]
            assert len(small) == N_CONST
            load(meta_nat[:], meta_tokens_2).then_inc(meta_in, 16)
            for dst, src in small:
                load(dst, src).then_inc(c_in, 16)
            load(masks[:], level_masks).then_inc(mask_in, 16)

            def level_add(level, i):
                pool.wait_ge(hg_m, 2 * level + i + 1)
                half = slice(8 * i, 8 * i + 8)
                tt(acc[:, half, :], acc[:, half, :], masked[:, half, :], ALU.add).then_inc(hg_acc, 1)

            def k_decay(level):
                hb = 2 ** (level - 1)
                n = HG * T // (2 * hb)
                src, dst = (g_even, g_odd)[(level - 1) % 2], (g_even, g_odd)[level % 2]
                pool.wait_ge(hg_s, level + 1)
                if level >= 2:
                    pool.wait_ge(hg_g, level - 1)
                pool.wait_ge(hg_q, level)
                pair = src[:, 0:2 * n].rearrange("p (n two) -> p n two", two=2)
                if level < LEVELS - 2:
                    tt(dst[:, 0:n], pair[:, :, 0], pair[:, :, 1], ALU.mult).then_inc(hg_g, 1)
                v = kr[:].rearrange("p n t -> p (n t)").rearrange("p (n two h) -> p n two h", two=2, h=hb)[:, :, 0, :]
                tt(v, v, spread(src[:, 1:2], [2, n], [0, hb]), ALU.mult).then_inc(hg_k, 1)

            def bias_load(j):
                if j == 0:
                    pool.wait_ge(hg_m, 2 * LEVELS)
                if j >= 2:
                    pool.wait_ge(at_nm, 2 * (j - 1))
                src = bass.AP(rel_bias.tensor, rel_bias.offset + 2 * j * N_REL + REL_CLIP + P - (T - 1),
                              [[1, P], [N_REL, 2], [1, T]])
                load(rel[:, j % 2, :, :], src).then_inc(rel_in[j % 2], 16)
                pool.wait_ge(rel_in[j % 2], 16 * (j // 2 + 1))
                nc.gpsimd.memset(rel[0:DH, j % 2, :, 0:DH], MASKED).then_inc(rel_ready, 1)

            for g in range(G_IN):
                if G_LEVEL < g < G_HGOUT - 1:
                    level = g - G_LEVEL
                    for i in range(2):
                        level_add(level, i)
                    k_decay(level)
                if g == G_HGOUT:
                    for i in range(4):
                        pool.wait_ge(hg_os, i + 1)
                        tt(o2_hg[:, 2 * i:2 * i + 2, :], o_hg[:, 2 * i:2 * i + 2, :], o_hg[:, 2 * i:2 * i + 2, :],
                           ALU.mult).then_inc(hg_o2, 1)
                if g == G_HGOUT + 1:
                    pool.wait_ge(hg_o2, 4)
                    for i in range(2):
                        tt(o_hg[:, 4 * i:4 * i + 4, :], o_hg[:, 4 * i:4 * i + 4, :], sg[:, 4 * i:4 * i + 4, :],
                           ALU.mult).then_inc(hg_t, 1)
                    bias_load(0)
                if g >= G_ATT:
                    for k in range(NC):
                        slot, odd = divmod(NC * (g - G_ATT) + k, 2)
                        if not odd and slot < AH and slot % 2 == 0 and slot // 2 + 1 < AH // 2:
                            bias_load(slot // 2 + 1)

            with pool.Fori(0, 4) as n:
                pool.wait_ge(set_free[1], G_IN // 2 + n + 1)
                tt(both[:], part_a[:], part_b[:], ALU.add).then_inc(br_m, 1)
            pool.wait_ge(br_ready, 4)
            load(fin_w[:], row_all(norm_final_w, D)).then_inc(finw_in, 16)
            with pool.Fori(0, QUARTERS) as q:
                for g in range(4):
                    pool.wait_ge(set_free[g % 2], G_IN // 2 + 6 + 4 * q + g // 2 + 1)
                    tt(relu2[:], relu[:], relu[:], ALU.mult).then_inc(up_sq, 1)

            def rope(n):
                pool.wait_ge(nr_rot, n + 1)
                w = TM if n == 0 else T
                nb = 2 if n == 0 else 4
                dst = ka[:] if n == 0 else qa[:, 4 * (n - 1):4 * n, :]
                v, r, q = qg[:, 0:nb, 0:w], qrot[:, 0:nb, 0:w], qsq[:, 0:nb, 0:w]
                tt(v, v, spread(cos_t[:], [0, nb], [1, w]), ALU.mult).then_inc(nr_cos, 1)
                pool.wait_ge(nr_cos, 2 * n + 1)
                pool.wait_ge(set_free[(1, 0, 1)[n]], rope_free[n])
                tt(v, v, r, ALU.add).then_inc(nr_cos, 1)
                pool.wait_ge(nr_cos, 2 * n + 2)
                pool.wait_ge(nr_rs, n + 1)
                tt(dst, v, q, ALU.mult).then_inc(nr_done, 1)

            def side(pos):
                if pos == POS_BN - 1:
                    pool.wait_ge(b_o, B_UNITS)
                    tt(ob2[:], ob[:], ob[:], ALU.mult).then_inc(bn_o2, 1)

            rope_free = (SETS_BEFORE_2 + 4, need2[7] + 1, need2[8] + 1)
            for j in range(G_IN2):
                for k in range(NC):
                    for n, jn in enumerate((5, 8, 9)):
                        if j == jn and k == 5:
                            rope(n)
                    if j >= J_B:
                        side(NC * (j - J_B) + k)
            for pos in range(NC * (G_IN2 - J_B), POS_A + A_SLOTS):
                side(pos)
            pool.wait_ge(bn_rs, 1)
            tt(ob[:], ob[:], obr[:], ALU.mult).then_inc(pool_step, 1)
            pool.wait_ge(pool_step, 1)
            tt(ob[:], ob[:], gb[:], ALU.mult).then_inc(bn_y, 1)
            pool.wait_ge(a_o, A_UNITS)
            pool.wait_ge(set_free[0], sets_before_out2[0])
            pool.wait_ge(set_free[1], sets_before_out2[1])
            tt(oa[:], oa[:], ga[:], ALU.mult).then_inc(an_y, 1)
            pool.wait_ge(bn_y, 1)
            load(post_w[:], row_all(post_norm_g_2, D)).then_inc(postw_in, 16)


_NAMES = ("x", "w_in", "lb_logits", "hg_norm_w", "rel_bias", "w_branch_a", "w_branch_b", "w_out", "norm_mix_w",
          "norm_mlp_w", "w_up", "w_down", "norm_final_w", "meta_tokens_2", "pre_norm_g_2", "w_in_2", "q_norm_g_2",
          "k_norm_g_2", "lambda_q1_2", "lambda_k1_2", "lambda_q2_2", "lambda_k2_2", "subln_g_2", "w_out_2",
          "post_norm_g_2")


def shape_constants():
    f32 = np.float32
    identity = np.eye(P, dtype=f32)
    s, t = np.arange(P)[:, None], np.arange(P)[None, :]
    masks = np.zeros((P, 8, P), f32)
    masks[:, 0, :] = s == t
    for level in range(1, 8):
        hb = 2 ** (level - 1)
        masks[:, level, :] = (s // (2 * hb) == t // (2 * hb)) & ((s // hb) % 2 == 0) & ((t // hb) % 2 == 1)
    inv_freq = (f32(10000.0) ** (-np.arange(0, DH, 2, dtype=f32) / f32(DH))).astype(f32)
    row = np.concatenate([np.arange(T) // 64, np.zeros(META, int)]).astype(f32)
    col = np.concatenate([np.arange(T) % 64, np.zeros(META, int)]).astype(f32)
    ang = np.stack([row[:, None] * inv_freq, col[:, None] * inv_freq]).astype(f32)
    half = np.concatenate([ang[0], ang[0], ang[1], ang[1]], axis=1).T
    rope_cos, rope_sin = np.cos(half).astype(f32), np.sin(half).astype(f32)
    turn = np.zeros((P, P), f32)
    for m in range(P):
        if (m // 32) % 2 == 0:
            turn[m + 32, m] = -1.0
        else:
            turn[m - 32, m] = 1.0
    qpos = np.arange(T) + META
    kpos = np.concatenate([np.arange(T) + META, np.arange(META)])
    distance = np.abs(qpos[:, None] - kpos[None, :]).astype(f32)
    return {"identity": identity, "level_masks": masks, "rope_cos": rope_cos, "rope_sin": rope_sin,
            "rope_turn": turn, "distance": distance}


def kernel(**inputs):
    import concourse.bacc as bacc
    from concourse.bass_utils import run_bass_kernel_spmd

    nc = bacc.Bacc("TRN2", target_bir_lowering=False, num_devices=1)
    arrays, args = {}, []
    for name, a in [(n, inputs[n]) for n in _NAMES] + list(shape_constants().items()):
        a = np.ascontiguousarray(a)
        arrays[f"in_{name}_dram"] = a
        args.append(nc.dram_tensor(f"in_{name}_dram", a.shape, mybir.dt.from_np(a.dtype), kind="ExternalInput").ap())
    out = nc.dram_tensor("out_0_dram", (1, T, D), F32, kind="ExternalOutput").ap()
    program(nc, *args, out)
    r = run_bass_kernel_spmd(nc, [arrays], core_ids=[0])
    return r.results[0]["out_0_dram"]
```

```python
import math
from contextlib import ExitStack

import numpy as np

import concourse.bass as bass
from concourse import mybir

ACT = mybir.ActivationFunctionType
ALU = mybir.AluOpType
AX = mybir.AxisListType
F32 = mybir.dt.float32
F32R = mybir.dt.float32r

P = 128
D = 2048
T = 256
NT = T // P
META = 16
TM = T + META
KT = D // P
HG = 8
AH = 16
DH = 64
N_REL = 513
REL_CLIP = 256
H2 = 8
KV2 = 2
EPS = 1e-6
MASKED = -1e30

CW = 512
CK = 2
NC = KT // CK
SLOTS = 4
LEAD = 4

C_IN = 0
G_IN = 22
C_BR = C_IN + G_IN * NC
C_OUT = C_BR + 4 * NC
C_FF = C_OUT + 4 * NC
QUARTERS = 4
C_IN2 = C_FF + QUARTERS * 8 * NC
IN2_COLS = (3584, 4096, 4608, 5120, 1024, 2560, 3072, 0, 512, 5632, 6144, 1536, 2048)
G_IN2 = len(IN2_COLS)
C_OUT2 = C_IN2 + G_IN2 * NC
C_END = C_OUT2 + 4 * NC
SETS_BEFORE_2 = (G_IN + 8 + 4 + 32) // 2

LEVELS = 9
G_LEVEL = 5
G_HGOUT = G_LEVEL + LEVELS
G_ATT = 16
J_B = 6
B_UNITS = H2 * NT
UNITS = 2 * B_UNITS
POS_BN = 23
POS_A = 28

LAMBDA_INIT = 0.8 - 0.6 * math.exp(-0.3 * 0)
N_CONST = 16
E_STEP = {g: n for n, g in enumerate([0, 1, 2, 3, 6, 7])}
N_E1 = len(E_STEP)


def unit_at(pos):
    if 0 <= pos < B_UNITS:
        return pos
    if POS_A <= pos < POS_A + B_UNITS:
        return B_UNITS + pos - POS_A
    return None


def program(nc, x, w_in, lb_logits, hg_norm_w, rel_bias, w_branch_a, w_branch_b, w_out, norm_mix_w,
            norm_mlp_w, w_up, w_down, norm_final_w, meta_tokens_2, pre_norm_g_2, w_in_2, q_norm_g_2,
            k_norm_g_2, lambda_q1_2, lambda_k1_2, lambda_q2_2, lambda_k2_2, subln_g_2, w_out_2,
            post_norm_g_2, identity, level_masks, rope_cos, rope_sin, rope_turn, distance, out):
    with ExitStack() as ctx:
        def sb(name, shape, dt=F32):
            return ctx.enter_context(nc.sbuf_tensor(name, shape, dt))

        def sem(name):
            return ctx.enter_context(nc.semaphore(name))

        raw = sb("raw", [P, SLOTS, CK, CW])
        whi = sb("whi", [P, SLOTS, CK, CW], F32R)
        wlo = sb("wlo", [P, SLOTS, CK, CW], F32R)
        xhi = sb("xhi", [P, KT, TM], F32R)
        xlo = sb("xlo", [P, KT, TM], F32R)
        ident = sb("ident", [P, P])
        ones = sb("ones", [P, P])
        mix_w = sb("mix_w", [P, KT])
        mlp_w = sb("mlp_w", [P, KT])
        pre_w = sb("pre_w", [P, KT])
        lbt = sb("lbt", [P, 2, HG])
        lbe = sb("lbe", [P, 2, HG])
        lbs = sb("lbs", [P, 4, HG])
        gvec = sb("gvec", [P, 4])
        subg = sb("subg", [P, 1])
        lamv = sb("lamv", [P, 4, DH])
        lams = sb("lams", [P, 8])
        eps_t = sb("eps_t", [P, 1])
        ss = sb("ss", [P, 16])
        sq = sb("sq", [P, 3, NT, 4])
        rstd = sb("rstd", [P, 16])
        nm = sb("nm", [P, 4, 2])
        rsum = sb("rsum", [P, 4, 2])
        rinv = sb("rinv", [P, 4, 2])
        cos_t = sb("cos_t", [P, TM])
        sin_t = sb("sin_t", [P, TM])
        turn = sb("turn", [P, P])
        dist = sb("dist", [P, NT, TM])
        ps = ctx.enter_context(nc.psum_tensor("ps", [P, 8, 512], F32))

        def at(name, kib, shape, dt=F32):
            with ExitStack() as tmp:
                if kib:
                    tmp.enter_context(nc.sbuf_tensor(name + "_pad", [P, int(kib * 256)], F32))
                return tmp.enter_context(nc.sbuf_tensor(name, shape, dt))

        x_nat = at("x_nat", 32, [P, NT, D])
        meta_nat = at("meta_nat", 80, [META, D])
        junk = at("junk", 72, [P, D])
        junk_b = at("junk_b", 108, [P, D])
        junk3 = at("junk3", 56, [P, D])
        junk3_b = at("junk3_b", 64, [P, D])
        meta_t = at("meta_t", 88, [P, KT, META])
        qp = at("qp", 16, [P, HG, T])
        v_hg = at("v_hg", 24, [P, NT, HG * P])
        aq = at("aq", 32, [P, HG, T])
        ak = at("ak", 40, [P, HG, T])
        av = at("av", 48, [P, NT, AH * DH])
        g_even = at("g_even", 56, [P, HG * T])
        g_odd = at("g_odd", 64, [P, HG * T // 2])
        cross = at("cross", 56, [P, HG, P])
        acc = at("acc", 68, [P, HG * NT, P])
        masked = at("masked", 76, [P, HG * NT, P])
        kr = at("kr", 88, [P, HG, T])
        sg = at("sg", 96, [P, HG, T])
        masks = at("masks", 104, [P, 8, P])
        o_hg = at("o_hg", 88, [P, HG, T])
        o2_hg = at("o2_hg", 76, [P, HG, T])
        rs_hg = at("rs_hg", 80, [P, HG, T])
        ya_hi = at("ya_hi", 0, [P, 8, T], F32R)
        ya_lo = at("ya_lo", 8, [P, 8, T], F32R)
        yb_hi = at("yb_hi", 16, [P, 8, T], F32R)
        yb_lo = at("yb_lo", 24, [P, 8, T], F32R)
        gates = at("gates", 56, [P, 32, T])
        rel = at("rel", 104, [P, 2, 2, T])
        prob = at("prob", 108, [P, 3, 3 * P])
        prob_t = at("prob_t", 112.5, [P, 2, 3 * P])
        part_a = at("part_a", 88, [P, 4, T])
        part_b = at("part_b", 92, [P, 4, T])
        both = at("both", 96, [P, 4, T])
        h = at("h", 32, [P, NT, D])
        normed = at("normed", 56, [P, NT, D])
        relu = at("relu", 88, [P, 4, T])
        relu2 = at("relu2", 96, [P, 4, T])
        fin_w = at("fin_w", 80, [P, D])
        kb = at("kb", 0, [P, H2, TM])
        qb = at("qb", 8.5, [P, H2, T])
        v_nat = at("v_nat", 17, [P, 10, NT, P])
        v_meta = at("v_meta", 27, [META, 10, P])
        ka = at("ka", 48, [P, KV2, TM])
        qa = at("qa", 51, [P, H2, T])
        v_t = at("v_t", 60, [P, 10, TM])
        oa = at("oa", 60, [P, H2, T])
        ob = at("ob", 68, [P, H2, T])
        pt2 = at("pt2", 76.5, [P, 2, 3 * P])
        ga = at("ga", 80, [P, H2, T])
        gb = at("gb", 88, [P, H2, T])
        qg = at("qg", 96, [P, 4, TM])
        qsq = at("qsq", 100.25, [P, 4, TM])
        qrot = at("qrot", 104.5, [P, 4, TM])
        p2 = at("p2", 108.75, [P, 4, 2, TM])
        ob2 = at("ob2", 0, [P, H2, T])
        obr = at("obr", 8.5, [P, H2, T])
        yt_hi = [at("yt_a_hi", 17, [P, 8, T], F32R), at("yt_b_hi", 0, [P, 8, T], F32R)]
        yt_lo = [at("yt_a_lo", 51, [P, 8, T], F32R), at("yt_b_lo", 8.5, [P, 8, T], F32R)]
        y2 = at("y2", 60, [P, NT, D])
        post_w = at("post_w", 88, [P, D])
        junk2 = at("junk2", 96, [P, D])
        junk2_b = at("junk2_b", 104.5, [P, D])

        raw_in = [sem(f"raw_in{i}") for i in range(SLOTS)]
        whi_ready = sem("whi_ready")
        wlo_ready = sem("wlo_ready")
        pe_done = sem("pe_done")
        set_free = [sem(f"set_free{i}") for i in range(2)]
        kvb_free = sem("kvb_free")
        x_in = [sem("x_in0"), sem("x_in1")]
        ident_in, mixw_in, c_in, meta_in = [sem(n) for n in ("ident_in", "mixw_in", "c_in", "meta_in")]
        mask_in, h_in, finw_in, postw_in = [sem(n) for n in ("mask_in", "h_in", "finw_in", "postw_in")]
        rel_in = [sem("rel_in0"), sem("rel_in1")]
        rel_ready = sem("rel_ready")
        n_ss, n_sum, n_sd, n_rs, n_un0, n_un1, n_tr, n_hi = [sem(n) for n in (
            "n_ss", "n_sum", "n_sd", "n_rs", "n_un0", "n_un1", "n_tr", "n_hi")]
        x_ready = sem("x_ready")
        f_w, f_sq, f_un = sem("f_w"), sem("f_sq"), sem("f_un")
        h_ready = sem("h_ready")
        setup = sem("setup")
        lb_max, lb_exp, lam_sum, lam_exp = [sem(n) for n in ("lb_max", "lb_exp", "lam_sum", "lam_exp")]
        m_ss, m_sd, m_un, m_tr, m_hi, meta_ready, m_w = [sem(n) for n in ("m_ss", "m_sd", "m_un", "m_tr", "m_hi", "meta_ready", "m_w")]
        e_sig = sem("e_sig")
        dve_step = sem("dve_step")
        sp_turn = sem("sp_turn")
        hg_s, hg_m, hg_acc, hg_q, hg_k, hg_g = [sem(n) for n in ("hg_s", "hg_m", "hg_acc", "hg_q", "hg_k", "hg_g")]
        hg_o, hg_os, hg_o2, hg_ss, hg_sd, hg_rs, hg_t, hg_y, hg_hi, ya_ready = [sem(n) for n in (
            "hg_o", "hg_os", "hg_o2", "hg_ss", "hg_sd", "hg_rs", "hg_t", "hg_y", "hg_hi", "ya_ready")]
        at_s, at_nm, at_exp, at_p, at_t, at_pt, at_pv, at_hi, at_y = [sem(n) for n in (
            "at_s", "at_nm", "at_exp", "at_p", "at_t", "at_pt", "at_pv", "at_hi", "at_y")]
        br_m, br_hi, br_ready = sem("br_m"), sem("br_hi"), sem("br_ready")
        up_sq, up_hi, up_ready = [sem(n) for n in ("up_sq", "up_hi", "up_ready")]
        vt_t, vt_c = [sem("vt_t0"), sem("vt_t1")], [sem("vt_c0"), sem("vt_c1")]
        nr_ev, nr_ss, nr_sd, nr_rs, nr_rot, nr_sin, nr_cos, nr_done = [sem(n) for n in (
            "nr_ev", "nr_ss", "nr_sd", "nr_rs", "nr_rot", "nr_sin", "nr_cos", "nr_done")]
        u_s, u_nm, u_exp, u_p, u_t, u_pt, u_pv, u_o = [sem(n) for n in (
            "u_s", "u_nm", "u_exp", "u_p", "u_t", "u_pt", "u_pv", "u_o")]
        bn_o2, bn_ss, bn_sd, bn_rs, bn_n, bn_y, bn_hi, yb2_ready = [sem(n) for n in (
            "bn_o2", "bn_ss", "bn_sd", "bn_rs", "bn_n", "bn_y", "bn_hi", "yb2_ready")]
        an_y, an_hi, ya2_ready = sem("an_y"), sem("an_hi"), sem("ya2_ready")
        y_ss, y_sd, y_w, y_out, stored = [sem(n) for n in ("y_ss", "y_sd", "y_w", "y_out", "stored")]

        def tiles(w, lead=True):
            return (w[0] if lead else w).rearrange("(k p) n -> p k n", p=P)

        w_in_t, w_a_t, w_b_t = tiles(w_in), tiles(w_branch_a), tiles(w_branch_b)
        w_out_t, w_up_t, w_down_t = tiles(w_out), tiles(w_up), tiles(w_down)
        w_in2_t, w_out2_t = tiles(w_in_2), tiles(w_out_2)

        def pset(s):
            return ps[:, 2 * s:2 * s + 2, :].rearrange("p b (x c) -> p (b x) c", x=2)

        misc = ps[:, 4:8, :]

        def spread(a, *dims):
            return bass.AP(a.tensor, a.offset, [list(a.ap[0])] + [list(d) for d in dims])

        def row_all(w, n):
            return bass.AP(w.tensor, w.offset, [[0, P], [1, n]])

        def set_needs():
            n = [SETS_BEFORE_2 + 3] * 2
            need = {}
            for j in range(5, G_IN2):
                s = (j - 5) % 2
                need[j] = n[s]
                n[s] += 1
                if j == 5:
                    n[1] += 1
            return need, n

        need2, sets_before_out2 = set_needs()

        block = ctx.enter_context(nc.Block())

        @block.sync
        def _(sp):
            def chunk(c0, k, src):
                if not isinstance(c0, int) or c0 + k >= SLOTS:
                    sp.wait_ge(wlo_ready, c0 + k - SLOTS + 1)
                    sp.sem_inc(sp_turn, 1)
                sp.dma_start(raw[:, k % SLOTS], src).then_inc(raw_in[k % SLOTS], 16)

            def rows(w, k, cols):
                return w[:, CK * k:CK * k + CK, cols]

            sp.dma_start(ident[:], identity).then_inc(ident_in, 16)
            for t in range(NT):
                sp.dma_start(x_nat[:, t], x[0, t * P:(t + 1) * P, :]).then_inc(x_in[t], 16)
            for k in range(NC):
                chunk(C_IN, k, rows(w_in_t, k, slice(0, CW)))
            with sp.Fori(1, G_IN) as g:
                for k in range(NC):
                    chunk(C_IN + NC * g, k, rows(w_in_t, k, bass.ds(g * CW, CW)))
            sp.wait_ge(at_s, AH)
            sp.dma_start(h[:], x[0].rearrange("(t p) d -> p t d", p=P)).then_inc(h_in, 16)
            with sp.Fori(0, 4) as n:
                for k in range(NC):
                    w = w_a_t if k < NC // 2 else w_b_t
                    chunk(C_BR + NC * n, k, rows(w, k % (NC // 2), bass.ds(n * CW, CW)))
            with sp.Fori(0, 4) as n:
                for k in range(NC):
                    chunk(C_OUT + NC * n, k, rows(w_out_t, k, bass.ds(n * CW, CW)))
            with sp.Fori(0, QUARTERS) as q:
                with sp.Fori(0, 4) as n:
                    for k in range(NC):
                        chunk(C_FF + 8 * NC * q + NC * n, k, rows(w_up_t, k, bass.ds(q * D + n * CW, CW)))
                with sp.Fori(0, 4) as n:
                    for k in range(NC):
                        chunk(C_FF + 8 * NC * q + 4 * NC + NC * n, k,
                              w_down_t[:, bass.ds(q * KT + CK * k, CK), bass.ds(n * CW, CW)])
            for j, col in enumerate(IN2_COLS):
                for k in range(NC):
                    chunk(C_IN2 + NC * j, k, rows(w_in2_t, k, slice(col, col + CW)))
            with sp.Fori(0, 4) as n:
                for k in range(NC):
                    chunk(C_OUT2 + NC * n, k, rows(w_out2_t, (k + NC // 2) % NC, bass.ds(n * CW, CW)))
            for i in range(2 * NT):
                t, cols = i // 2, slice((i % 2) * (D // 2), (i % 2 + 1) * (D // 2))
                sp.wait_ge(y_out, i + 1)
                sp.dma_start(out[0, t * P:(t + 1) * P, cols], y2[:, t, cols]).then_inc(stored, 16)
            sp.wait_ge(stored, 32 * NT)

        @block.tensor
        def _(pe):
            mm = nc.tensor.matmul

            def chunk_t(c0, k, kt0, xh, xl, outs, n, first, last, shared=True):
                pe.wait_ge(wlo_ready, c0 + k + 1)
                for j in range(CK):
                    kt = kt0 + j
                    for b in range(4):
                        cols = slice(b * P, (b + 1) * P)
                        for i, (w, v) in enumerate(((whi, xh), (whi, xl), (wlo, xh))):
                            start = first and j == 0 and i == 0 and (b % 2 == 0 or not shared)
                            ins = mm(outs[b], w[:, k % SLOTS, j, cols], v[:, kt, 0:n], start=start,
                                     stop=last and j == CK - 1 and i == 2, skip_group_check=True)
                ins.then_inc(pe_done, 1)

            def chunk_n(c0, k, kt0, xh, xl, s, first, last):
                pe.wait_ge(wlo_ready, c0 + k + 1)
                for j in range(CK):
                    kt = kt0 + j
                    for t in range(NT):
                        toks = slice(t * P, (t + 1) * P)
                        for i, (v, w) in enumerate(((xh, whi), (xh, wlo), (xl, whi))):
                            ins = mm(ps[:, 2 * s + t, :], v[:, kt, toks], w[:, k % SLOTS, j, :],
                                     start=first and j == 0 and i == 0,
                                     stop=last and j == CK - 1 and i == 2, skip_group_check=True)
                ins.then_inc(pe_done, 1)

            def blocks(s):
                return [pset(s)[:, b, :] for b in range(4)]

            def turn_normed(b):
                for kt in range(KT):
                    if kt % 4 == 0:
                        pe.wait_ge(n_un0, 4 * b + kt // 4 + 1)
                        pe.wait_ge(n_un1, 4 * b + kt // 4 + 1)
                    if kt >= 8 and kt % 2 == 0:
                        pe.wait_ge(x_ready, KT * b + kt - 6)
                    for t in range(NT):
                        o = (kt % 2) * T + t * P
                        ins = nc.tensor.transpose(ps[:, 4 + (kt % 8) // 2, o:o + P],
                                                  normed[:, t, kt * P:(kt + 1) * P], ident[:])
                    if kt % 2 == 1:
                        ins.then_inc(n_tr, 1)

            def turn_meta():
                pe.wait_ge(m_un, 1)
                for kt in range(KT):
                    ins = nc.tensor.transpose(ps[:, 3, kt * META:(kt + 1) * META],
                                              meta_nat[:, kt * P:(kt + 1) * P], ident[0:META, 0:META])
                ins.then_inc(m_tr, 1)

            pe.wait_ge(ident_in, 16)
            turn_normed(0)

            def level_scores(level):
                pe.wait_ge(hg_m, 2 * level) if level else None
                if level:
                    pe.wait_ge(hg_q, level)
                if level > 1:
                    pe.wait_ge(hg_k, level - 1)
                if level < LEVELS - 1:
                    for i in range(HG * NT):
                        hd, toks = i // NT, slice((i % NT) * P, (i % NT + 1) * P)
                        ins = mm(misc[:, i // 4, (i % 4) * P:(i % 4 + 1) * P], kr[:, hd, toks],
                                 qp[:, hd, toks], start=True, stop=True)
                else:
                    for hd in range(HG):
                        ins = mm(misc[:, hd // 4, (hd % 4) * P:(hd % 4 + 1) * P], kr[:, hd, 0:P],
                                 qp[:, hd, P:T], start=True, stop=True)
                ins.then_inc(hg_s, 1)

            def hg_output():
                pe.wait_ge(hg_acc, 2 * (LEVELS - 2))
                pe.wait_ge(hg_m, 2 * LEVELS)
                for hd in range(HG):
                    cols = slice(hd * P, (hd + 1) * P)
                    o = (hd % 2) * T
                    mm(misc[:, hd // 2, o:o + P], v_hg[:, 0, cols], acc[:, NT * hd, :],
                       start=True, stop=True)
                    mm(misc[:, hd // 2, o + P:o + T], v_hg[:, 1, cols], acc[:, NT * hd + 1, :],
                       start=True, stop=False)
                    ins = mm(misc[:, hd // 2, o + P:o + T], v_hg[:, 0, cols], cross[:, hd, :],
                             start=False, stop=True)
                ins.then_inc(hg_o, 1)

            def hg_squares():
                pe.wait_ge(hg_os, 4)
                pe.wait_ge(hg_o2, 4)
                for i in range(4):
                    ins = mm(misc[:, i, :], ones[:], o2_hg[:, 2 * i:2 * i + 2, :], start=True, stop=True)
                ins.then_inc(hg_ss, 1)

            def att_scores(u):
                if u == 0:
                    pe.wait_ge(hg_sd, 4)
                else:
                    pe.wait_ge(at_nm, u)
                f = slice(DH * (u % 2), DH * (u % 2) + DH)
                mm(ps[:, 4, 0:P], aq[f, u // 2, 0:P], ak[f, u // 2, 0:P], start=True, stop=True)
                mm(ps[:, 4, P:3 * P], aq[f, u // 2, P:T], ak[f, u // 2, :],
                   start=True, stop=True).then_inc(at_s, 1)

            def att_turn(u):
                pe.wait_ge(at_p, 2 * (u + 1))
                if u >= 1:
                    pe.wait_ge(at_pt, u)
                for i in range(3):
                    ins = nc.tensor.transpose(ps[:, 5, i * P:(i + 1) * P],
                                              prob[:, u % 3, i * P:(i + 1) * P], ident[:])
                ins.then_inc(at_t, 1)

            def att_values(u):
                pe.wait_ge(at_pt, u + 1)
                if u >= 4 and u % 2 == 0:
                    pe.wait_ge(at_y, u // 2 - 1)
                o = ps[DH * (u % 2):DH * (u % 2) + DH, 6 + (u // 2) % 2, :]
                cols = slice(u * DH, (u + 1) * DH)
                mm(o[:, 0:T], av[:, 0, cols], prob_t[:, u % 2, 0:T], start=True, stop=True)
                mm(o[:, P:T], av[:, 1, cols], prob_t[:, u % 2, T:T + P],
                   start=False, stop=True, skip_group_check=True).then_inc(at_pv, 1)

            for g in range(G_IN):
                c0, s = C_IN + NC * g, g % 2
                if g >= 2:
                    pe.wait_ge(set_free[s], g // 2)
                if g == 1:
                    pe.wait_ge(meta_ready, 1)
                natural = g in (4, 5, 12, 13)
                for k in range(NC):
                    if g == 0:
                        pe.wait_ge(x_ready, CK * (k + 1))
                    if natural:
                        chunk_n(c0, k, CK * k, xhi, xlo, s, k == 0, k == NC - 1)
                    else:
                        chunk_t(c0, k, CK * k, xhi, xlo, blocks(s), T, k == 0, k == NC - 1)
                    if k == 5 and g == 0:
                        turn_meta()
                    if k == 1 and G_LEVEL <= g < G_HGOUT:
                        level_scores(g - G_LEVEL)
                    if k == 1 and g == G_HGOUT:
                        hg_output()
                    if k == 6 and g == G_HGOUT:
                        hg_squares()
                    slot, odd = divmod(NC * (g - G_ATT) + k, 2)
                    if g >= G_ATT and not odd and slot < AH + 3:
                        if slot >= 3:
                            att_values(slot - 3)
                        if 2 <= slot < AH + 2:
                            att_turn(slot - 2)
                        if slot < AH:
                            att_scores(slot)

            pe.wait_ge(ya_ready, 4)
            with pe.Fori(0, 4) as n:
                c0 = C_BR + NC * n
                for s, (yh, yl) in enumerate(((ya_hi, ya_lo), (yb_hi, yb_lo))):
                    pe.wait_ge(set_free[s], G_IN // 2 + n)
                    if s == 1:
                        pe.wait_ge(at_y, AH // 2)
                    for k in range(NC // 2):
                        chunk_t(c0, NC // 2 * s + k, CK * k, yh, yl, blocks(s), T, k == 0, k == NC // 2 - 1)

            with pe.Fori(0, 2) as i:
                for s in range(2):
                    pe.wait_ge(set_free[s], G_IN // 2 + 4 + i)
                    for k in range(NC):
                        pe.wait_ge(br_ready, k // 2 + 1)
                        chunk_n(C_OUT + 2 * NC * i + NC * s, k, CK * k, xhi, xlo, s, k == 0, k == NC - 1)

            turn_normed(1)

            def quarter(q):
                c0 = C_FF + 8 * NC * q
                for g in range(4):
                    pe.wait_ge(set_free[g % 2], G_IN // 2 + 6 + 4 * q + g // 2)
                    for k in range(NC):
                        if g == 0:
                            pe.wait_ge(x_ready, KT + CK * (k + 1))
                        chunk_t(c0 + NC * g, k, CK * k, xhi, xlo, blocks(g % 2), T, k == 0, k == NC - 1)
                for g in range(4):
                    pe.wait_ge(set_free[g % 2], G_IN // 2 + 8 + 4 * q + g // 2)
                    for k in range(NC):
                        pe.wait_ge(up_ready, 4 * q + k // 2 + 1)
                        uh, ul = (ya_hi, ya_lo) if k < NC // 2 else (yb_hi, yb_lo)
                        chunk_n(c0 + 4 * NC + NC * g, k, CK * (k % (NC // 2)), uh, ul, g % 2, k == 0, k == NC - 1)

            with pe.Fori(0, QUARTERS - 1) as q:
                quarter(q)
            quarter(QUARTERS - 1)

            turn_normed(2)

            def values_turn(b):
                if b < 4:
                    pe.wait_ge(kvb_free, 2)
                else:
                    pe.wait_ge(vt_c[b % 2], (b - 4) // 2 + 1)
                o = ps[:, 4 + b % 4, :]
                nc.tensor.transpose(o[:, 0:P], v_t[:, b, 0:P], ident[:])
                nc.tensor.transpose(o[:, P:T], v_t[:, b, P:T], ident[:])
                nc.tensor.transpose(o[0:META, T:T + P], v_t[:, b, T:TM], ident[:]).then_inc(vt_t[b % 2], 1)

            def rope_squares(n, s):
                pe.wait_ge(nr_ev, 2 * n + 1)
                if n == 0:
                    pe.wait_ge(set_free[0], SETS_BEFORE_2 + 3)
                    pe.wait_ge(set_free[1], SETS_BEFORE_2 + 3)
                for i in range(2):
                    src = qsq[:, i, :] if n == 0 else qsq[:, 2 * i:2 * i + 2, 0:T]
                    w = TM if n == 0 else 2 * T
                    ins = mm(ps[:, 2 * s + i, 0:w], ones[:], src, start=True, stop=True)
                ins.then_inc(nr_ss, 1)

            def rope_turn_halves(n, s):
                pe.wait_ge(nr_sd, n + 1)
                for i in range(2):
                    src = qg[:, i, :] if n == 0 else qg[:, 2 * i:2 * i + 2, 0:T]
                    w = TM if n == 0 else 2 * T
                    ins = mm(ps[:, 2 * s + i, 0:w], turn[:], src, start=True, stop=True)
                ins.then_inc(nr_rot, 1)

            def scores(u):
                hd, t = divmod(u % B_UNITS, NT)
                if u == 0:
                    for i in range(2):
                        pe.wait_ge(vt_c[i], 5)
                if u < B_UNITS:
                    if hd in (0, H2 // 2) and t == 0:
                        s = 0 if hd == 0 else 1
                        pe.wait_ge(set_free[s], need2[5 + s] + 1)
                    if u >= 1:
                        pe.wait_ge(u_nm, u)
                    for i in range(2):
                        f = slice(DH * i, DH * i + DH)
                        ins = mm(ps[:, 4 + i, 0:TM], qb[f, hd, t * P:(t + 1) * P], kb[f, hd, :],
                                 start=True, stop=True)
                    ins.then_inc(u_s, 1)
                else:
                    if hd in (0, H2 // 2) and t == 0:
                        pe.wait_ge(nr_done, 2 + hd // (H2 // 2))
                    if u == B_UNITS:
                        pe.wait_ge(bn_sd, 4)
                    if u >= B_UNITS + 2:
                        pe.wait_ge(u_exp, u - 1)
                    mm(ps[:, 4 + u % 2, 0:TM], qa[:, hd, t * P:(t + 1) * P], ka[:, hd // (H2 // KV2), :],
                       start=True, stop=True).then_inc(u_s, 1)

            def weights_turn(u):
                pe.wait_ge(u_p, u + 1)
                if u >= 1:
                    pe.wait_ge(u_pt, u)
                p = p2[:, u % 4, 0, :]
                nc.tensor.transpose(ps[:, 6, 0:P], p[:, 0:P], ident[:])
                nc.tensor.transpose(ps[:, 6, P:T], p[:, P:T], ident[:])
                nc.tensor.transpose(ps[0:META, 6, T:T + P], p[:, T:TM], ident[:]).then_inc(u_t, 1)

            def values(u):
                pe.wait_ge(u_pt, u + 1)
                if u >= 1:
                    pe.wait_ge(u_o, u)
                hd = u % B_UNITS // NT
                vh = hd if u < B_UNITS else 8 + hd // (H2 // KV2)
                mm(ps[:, 7, 0:P], v_nat[:, vh, 0, :], pt2[:, u % 2, 0:P], start=True, stop=False)
                mm(ps[:, 7, 0:P], v_nat[:, vh, 1, :], pt2[:, u % 2, P:T], start=False, stop=False)
                mm(ps[:, 7, 0:P], v_meta[:, vh, :], pt2[0:META, u % 2, T:T + P], start=False,
                   stop=True).then_inc(u_pv, 1)

            def b_norm_squares():
                pe.wait_ge(bn_o2, 1)
                pe.wait_ge(u_o, B_UNITS)
                for i in range(4):
                    mm(ps[:, 4 + i, :], ones[:], ob2[:, 2 * i:2 * i + 2, :], start=True,
                       stop=True).then_inc(bn_ss, 1)

            def side(pos):
                if unit_at(pos - 4) is not None:
                    values(unit_at(pos - 4))
                if unit_at(pos - 3) is not None:
                    weights_turn(unit_at(pos - 3))
                if unit_at(pos) is not None:
                    scores(unit_at(pos))
                if pos == POS_BN:
                    b_norm_squares()

            pe.wait_ge(c_in, 16 * N_CONST)
            for j in range(G_IN2):
                c0 = C_IN2 + NC * j
                kv = j < 5
                if kv and j % 2 == 0:
                    for s in range(2):
                        pe.wait_ge(set_free[s], SETS_BEFORE_2 + j // 2)
                    outs = [ps[:, b, 0:TM] for b in range(4)]
                elif kv:
                    if j == 3:
                        pe.wait_ge(kvb_free, 1)
                    outs = [ps[:, 4 + b, 0:TM] for b in range(4)]
                else:
                    s = (j - 5) % 2
                    pe.wait_ge(set_free[s], need2[j])
                    outs = blocks(s)
                for k in range(NC):
                    if j == 0:
                        pe.wait_ge(x_ready, 2 * KT + CK * (k + 1))
                    chunk_t(c0, k, CK * k, xhi, xlo, outs, TM if kv else T, k == 0, k == NC - 1, shared=not kv)
                    if j == 5 and 1 <= k <= 5:
                        values_turn(2 * (k - 1))
                        values_turn(2 * (k - 1) + 1)
                    for n, jn in enumerate((5, 8, 9)):
                        if j == jn and k == 1:
                            rope_squares(n, (1, 0, 1)[n])
                        if j == jn and k == 4:
                            rope_turn_halves(n, (1, 0, 1)[n])
                    if j >= J_B:
                        side(NC * (j - J_B) + k)

            with pe.Fori(0, 2) as i:
                for s in range(2):
                    pe.wait_ge(set_free[s], sets_before_out2[s] + i)
                    for k in range(NC):
                        mixer = 1 if k < NC // 2 else 0
                        pe.wait_ge((ya2_ready, yb2_ready)[mixer], 1 + k % (NC // 2) // 2)
                        chunk_n(C_OUT2 + 2 * NC * i + NC * s, k, CK * (k % (NC // 2)), yt_hi[mixer], yt_lo[mixer],
                                s, k == 0, k == NC - 1)

        @block.scalar
        def _(act):
            f = nc.scalar.activation

            def split_hi(c0, k):
                act.wait_ge(raw_in[k % SLOTS], 4 * c0 + 16 * (k // SLOTS + 1))
                if not isinstance(c0, int) or c0 + k >= SLOTS:
                    act.wait_ge(pe_done, c0 + k - SLOTS + 1)
                f(whi[:, k % SLOTS], raw[:, k % SLOTS], ACT.Copy).then_inc(whi_ready, 1)

            def square(part, n, src, junk_, t, done):
                f(junk_, src, ACT.Square, accum_out=sq[:, part, t, n:n + 1]).then_inc(done, 1)

            def norm(b, src, w, col):
                act.wait_ge(n_sum, b + 1)
                f(ss[:, col:col + 2], ss[:, col:col + 2], ACT.Sqrt, bias=eps_t[:], scale=1.0 / D).then_inc(n_sd, 1)
                act.wait_ge(n_rs, b + 1)
                for i in range(4):
                    cols = slice(i * CW, (i + 1) * CW)
                    f(normed[:, 1, cols], src[:, 1, cols], ACT.Copy, scale=rstd[:, col + 1:col + 2]).then_inc(n_un1, 1)
                for kt in range(KT):
                    act.wait_ge(n_tr, KT // 2 * b + kt // 2 + 1)
                    f(xhi[:, kt, 0:T], ps[:, 4 + (kt % 8) // 2, (kt % 2) * T:(kt % 2) * T + T], ACT.Copy,
                      scale=w[:, kt:kt + 1]).then_inc(n_hi, 1)

            for t in range(NT):
                act.wait_ge(x_in[t], 16)
                for i in range(4):
                    cols = slice(i * CW, (i + 1) * CW)
                    square(0, i, x_nat[:, t, cols], junk[:, cols] if t == 0 else junk_b[:, cols], t, n_ss)
            act.wait_ge(setup, 1)
            act.wait_ge(mixw_in, 16)
            norm(0, x_nat, mix_w, 0)
            for k in range(LEAD):
                split_hi(C_IN, k)

            def start_meta():
                act.wait_ge(meta_in, 16)
                act.wait_ge(n_hi, KT)
                f(junk[0:META, :], meta_nat[:], ACT.Square, accum_out=ss[0:META, 8:9]).then_inc(m_ss, 1)
                act.wait_ge(m_ss, 1)
                f(ss[0:META, 8:9], ss[0:META, 8:9], ACT.Sqrt, bias=eps_t[0:META], scale=1.0 / D).then_inc(m_sd, 1)
                act.wait_ge(lb_max, 1)
                f(lbe[:], lbt[:], ACT.Exp).then_inc(lb_exp, 1)
                act.wait_ge(lam_sum, 1)
                f(lams[:, 2:4], lams[:, 0:2], ACT.Exp).then_inc(lam_exp, 1)

            def sigmoid(dst, s, done):
                f(dst, pset(s), ACT.Sigmoid).then_inc(done, 1)

            def evac_in(g):
                act.wait_ge(pe_done, C_IN + NC * (g + 1))
                s, half = g % 2, slice(4 * (g % 2), 4 * (g % 2) + 4)
                if g < 2:
                    sigmoid(qp[:, half, :], s, e_sig)
                elif g < 4:
                    sigmoid(g_even[:].rearrange("p (n t) -> p n t", t=T)[:, half, :], s, e_sig)
                elif g < 6:
                    f(v_hg[:, :, (g % 2) * CW:(g % 2 + 1) * CW], ps[:, 2 * s:2 * s + 2, :],
                      ACT.Copy).then_inc(set_free[s], 1)
                elif g < 8:
                    sigmoid(sg[:, half, :], s, e_sig)
                elif g < 10:
                    f(aq[:, half, :], pset(s), ACT.Copy, scale=DH ** -0.5).then_inc(set_free[s], 1)
                elif g < 12:
                    f(ak[:, half, :], pset(s), ACT.Copy).then_inc(set_free[s], 1)
                elif g < 14:
                    f(av[:, :, (g % 2) * CW:(g % 2 + 1) * CW], ps[:, 2 * s:2 * s + 2, :],
                      ACT.Copy).then_inc(set_free[s], 1)
                else:
                    sigmoid(gates[:, 4 * (g - 14):4 * (g - 14) + 4, :], s, set_free[s])

            def hg_copy(i):
                act.wait_ge(hg_o, 1)
                f(o_hg[:, 2 * i:2 * i + 2, :], misc[:, i, :].rearrange("p (x c) -> p x c", x=2),
                  ACT.Copy).then_inc(hg_os, 1)

            def hg_root(i):
                act.wait_ge(hg_ss, 1)
                f(rs_hg[:, 2 * i:2 * i + 2, :], misc[:, i, :].rearrange("p (x c) -> p x c", x=2), ACT.Sqrt,
                  bias=eps_t[:], scale=1.0 / P).then_inc(hg_sd, 1)

            def hg_upper(i):
                act.wait_ge(hg_y, i + 1)
                f(ya_hi[:, 2 * i:2 * i + 2, :], o_hg[:, 2 * i:2 * i + 2, :], ACT.Copy).then_inc(hg_hi, 1)

            def att_exp(u):
                act.wait_ge(at_nm, u + 1)
                for t, cols in enumerate((slice(0, P), slice(P, 3 * P))):
                    f(prob[:, u % 3, cols], prob[:, u % 3, cols], ACT.Exp, bias=nm[:, u % 3, t:t + 1],
                      scale=-1.0, accum_out=rsum[:, u % 3, t:t + 1]).then_inc(at_exp, 1)

            def att_copy(u):
                act.wait_ge(at_t, u + 1)
                if u >= 2:
                    act.wait_ge(at_pv, u - 1)
                f(prob_t[:, u % 2, :], ps[:, 5, 0:3 * P], ACT.Copy).then_inc(at_pt, 1)

            def att_upper(j):
                act.wait_ge(at_pv, 2 * (j + 1))
                f(yb_hi[:, j, :], ps[:, 6 + j % 2, 0:T], ACT.Copy).then_inc(at_hi, 1)

            for g in range(G_IN):
                for k in range(NC):
                    split_hi(C_IN + NC * g, LEAD + k)
                    if g == 0 and k == 2:
                        start_meta()
                    if g == 0 and k == 6:
                        act.wait_ge(m_w, 1)
                        f(xhi[:, :, T:TM], meta_t[:], ACT.Copy).then_inc(m_hi, 1)
                    if g == G_HGOUT and 2 <= k <= 5:
                        hg_copy(k - 2)
                    if g == G_HGOUT and k == 7:
                        for i in range(4):
                            hg_root(i)
                    if g == G_HGOUT + 3 and k % 2 == 0:
                        hg_upper(k // 2)
                    slot, odd = divmod(NC * (g - G_ATT) + k, 2)
                    if g >= G_ATT and odd and slot < AH + 3:
                        if 2 <= slot < AH + 2:
                            att_copy(slot - 2)
                        if slot < AH:
                            att_exp(slot)
                        if slot >= 4 and slot % 2 == 0:
                            att_upper((slot - 4) // 2)
                evac_in(g)

            with act.Fori(0, 4) as n:
                for k in range(NC):
                    split_hi(C_BR + NC * n, LEAD + k)
                act.wait_ge(br_m, n + 1)
                f(xhi[:, bass.ds(4 * n, 4), 0:T], both[:], ACT.Copy).then_inc(br_hi, 1)
            def h_squares(part, n, free, done):
                act.wait_ge(set_free[n % 2], free)
                for t in range(NT):
                    cols = slice(n * CW, (n + 1) * CW)
                    square(part, n, h[:, t, cols], (junk, junk_b)[t][:, cols], t, done)

            for n in range(4):
                for k in range(NC):
                    split_hi(C_OUT + NC * n, LEAD + k)
                h_squares(1, n, G_IN // 2 + 4 + n // 2 + 1, n_ss)
            norm(1, h, mlp_w, 2)

            def quarter(q, last):
                c0 = C_FF + 8 * NC * q
                for g in range(4):
                    for k in range(NC):
                        split_hi(c0 + NC * g, LEAD + k)
                    act.wait_ge(pe_done, c0 + NC * (g + 1))
                    f(relu[:], pset(g % 2), ACT.Relu).then_inc(set_free[g % 2], 1)
                    act.wait_ge(up_sq, 4 * q + g + 1)
                    dst = (ya_hi, yb_hi)[g // 2]
                    f(dst[:, 4 * (g % 2):4 * (g % 2) + 4, :], relu2[:], ACT.Copy).then_inc(up_hi, 1)
                for g in range(4):
                    for k in range(NC):
                        split_hi(c0 + 4 * NC + NC * g, LEAD + k)
                    if last:
                        h_squares(1, g, G_IN // 2 + 8 + 4 * q + g // 2 + 1, f_sq)
                        act.wait_ge(f_w, g + 1)
                        for t in range(NT):
                            cols = slice(g * CW, (g + 1) * CW)
                            square(2, g, h[:, t, cols], (junk3, junk3_b)[t][:, cols], t, n_ss)

            with act.Fori(0, QUARTERS - 1) as q:
                quarter(q, False)
            quarter(QUARTERS - 1, True)
            act.wait_ge(f_un, 1)
            f(ss[:, 4:6], ss[:, 4:6], ACT.Sqrt, bias=eps_t[:], scale=1.0 / D).then_inc(f_un, 1)
            norm(2, h, pre_w, 6)

            def evac_in2(j):
                act.wait_ge(pe_done, C_IN2 + NC * (j + 1))
                if j in (0, 2):
                    for s in range(2):
                        dst = kb if j == 0 else v_t
                        f(dst[:, (0 if j == 0 else 0) + 2 * s:2 * s + 2, :], ps[:, 2 * s:2 * s + 2, 0:TM],
                          ACT.Copy).then_inc(set_free[s], 1)
                elif j in (1, 3):
                    dst = kb if j == 1 else v_t
                    f(dst[:, 4:8, :], ps[:, 4:8, 0:TM], ACT.Copy).then_inc(kvb_free, 1)
                elif j == 4:
                    f(qg[:, 0:2, :], ps[:, 0:2, 0:TM], ACT.Copy, scale=gvec[:, 2:3]).then_inc(nr_ev, 1)
                    f(qsq[:, 0:2, :], ps[:, 0:2, 0:TM], ACT.Square).then_inc(set_free[0], 1)
                    f(v_t[:, 8:10, :], ps[:, 2:4, 0:TM], ACT.Copy).then_inc(set_free[1], 1)
                elif j in (5, 6):
                    s = (j - 5) % 2
                    f(qb[:, 4 * s:4 * s + 4, :], pset(s), ACT.Copy, scale=DH ** -0.5).then_inc(set_free[s], 1)
                elif j in (7, 8):
                    n = j - 6
                    act.wait_ge(nr_done, n)
                    f(qg[:, :, 0:T], pset(n - 1), ACT.Copy, scale=gvec[:, 1:2]).then_inc(nr_ev, 1)
                    f(qsq[:, :, 0:T], pset(n - 1), ACT.Square).then_inc(nr_ev, 1)
                else:
                    g = (j - 9)
                    dst = gb if g < 2 else ga
                    sigmoid(dst[:, 4 * (g % 2):4 * (g % 2) + 4, :], g % 2, e_sig)

            def values_copy(b):
                act.wait_ge(vt_t[1], b // 2 + 1)
                f(v_nat[:, b, :, :], ps[:, 4 + b % 4, 0:T].rearrange("p (t c) -> p t c", t=2), ACT.Copy)
                f(v_meta[:, b, :], ps[0:META, 4 + b % 4, T:T + P], ACT.Copy).then_inc(vt_c[1], 1)

            def rope_root(n, s):
                act.wait_ge(nr_ss, n + 1)
                if n == 0:
                    dst, src = qsq[:, 0:2, :], ps[:, 2 * s:2 * s + 2, 0:TM]
                else:
                    dst, src = qsq[:, :, 0:T], pset(s)
                f(dst, src, ACT.Sqrt, bias=eps_t[:], scale=1.0 / P).then_inc(nr_sd, 1)

            def unit_exp(u):
                act.wait_ge(u_nm, u + 1)
                if u < B_UNITS:
                    for i in range(2):
                        ins = f(p2[:, u % 4, i, :], p2[:, u % 4, i, :], ACT.Exp, bias=nm[:, u % 4, i:i + 1],
                                scale=-1.0, accum_out=rsum[:, u % 4, i:i + 1])
                else:
                    ins = f(p2[:, u % 4, 0, :], ps[:, 4 + u % 2, 0:TM], ACT.Exp, bias=nm[:, u % 4, 0:1],
                            scale=P ** -0.5, accum_out=rsum[:, u % 4, 0:1])
                ins.then_inc(u_exp, 1)

            def unit_copy(u):
                act.wait_ge(u_t, u + 1)
                if u >= 2:
                    act.wait_ge(u_pv, u - 1)
                f(pt2[:, u % 2, 0:T], ps[:, 6, 0:T], ACT.Copy)
                f(pt2[0:META, u % 2, T:T + P], ps[0:META, 6, T:T + P], ACT.Copy).then_inc(u_pt, 1)

            def side(pos):
                if unit_at(pos - 3) is not None:
                    unit_copy(unit_at(pos - 3))
                if unit_at(pos - 1) is not None:
                    unit_exp(unit_at(pos - 1))
                if POS_BN < pos <= POS_BN + 4:
                    i = pos - POS_BN - 1
                    act.wait_ge(bn_ss, i + 1)
                    f(obr[:, 2 * i:2 * i + 2, :], ps[:, 4 + i, :].rearrange("p (x c) -> p x c", x=2), ACT.Sqrt,
                      bias=eps_t[:], scale=1.0 / P).then_inc(bn_sd, 1)

            def y_upper(mixer, i, src, ready, done):
                act.wait_ge(ready, i + 1)
                f(yt_hi[mixer][:, 4 * i:4 * i + 4, :], src[:, 4 * i:4 * i + 4, :], ACT.Copy).then_inc(done, 1)

            for j in range(G_IN2):
                for k in range(NC):
                    split_hi(C_IN2 + NC * j, LEAD + k)
                    if j == 5 and 2 <= k <= 6:
                        values_copy(2 * (k - 2) + 1)
                    for n, jn in enumerate((5, 8, 9)):
                        if j == jn and k == 2:
                            rope_root(n, (1, 0, 1)[n])
                    if j >= J_B:
                        side(NC * (j - J_B) + k)
                    if j == G_IN2 - 1 and k in (1, 3):
                        y_upper(1, k // 2, ob, bn_y, bn_hi)
                    if j == G_IN2 - 1 and k == 5:
                        act.wait_ge(u_pv, UNITS)
                        y_upper(0, 0, oa, an_y, an_hi)
                evac_in2(j)
            y_upper(0, 1, oa, an_y, an_hi)
            for g in range(4):
                for k in range(NC):
                    if NC * g + LEAD + k < 4 * NC:
                        split_hi(C_OUT2 + NC * g, LEAD + k)
                act.wait_ge(pe_done, C_OUT2 + NC * (g + 1))
                cols = slice(g * CW, (g + 1) * CW)
                square(0, g, ps[:, 2 * (g % 2), :], junk2[:, cols], 0, y_ss)
                act.wait_ge(y_w, g + 1)
                square(0, g, ps[:, 2 * (g % 2) + 1, :], junk2_b[:, cols], 1, y_ss)
            act.wait_ge(y_sd, 1)
            f(ss[:, 10:12], ss[:, 10:12], ACT.Sqrt, bias=eps_t[:], scale=1.0 / D).then_inc(y_sd, 1)

        @block.vector
        def _(dve):
            tt, ts, stt = nc.vector.tensor_tensor, nc.vector.tensor_scalar, nc.vector.scalar_tensor_tensor
            steps = [0]

            def own(ins):
                steps[0] += 1
                ins.then_inc(dve_step, 1)
                dve.wait_ge(dve_step, steps[0])

            def split_lo(c0, k):
                dve.wait_ge(whi_ready, c0 + k + 1)
                tt(wlo[:, k % SLOTS], raw[:, k % SLOTS], whi[:, k % SLOTS], ALU.subtract).then_inc(wlo_ready, 1)

            def norm(b, src, w, col):
                dve.wait_ge(n_sd, b + 1)
                nc.vector.reciprocal(rstd[:, col:col + 2], ss[:, col:col + 2]).then_inc(n_rs, 1)
                norm_tail(b, src, w, col)

            def norm_tail(b, src, w, col):
                dve.wait_ge(n_rs, b + 1)
                for i in range(4):
                    cols = slice(i * CW, (i + 1) * CW)
                    ts(normed[:, 0, cols], src[:, 0, cols], rstd[:, col:col + 1], None, ALU.mult).then_inc(n_un0, 1)
                for kt in range(KT):
                    dve.wait_ge(n_hi, KT * b + kt // 2 * 2 + 2)
                    stt(out=xlo[:, kt, 0:T], in0=ps[:, 4 + (kt % 8) // 2, (kt % 2) * T:(kt % 2) * T + T],
                        scalar=w[:, kt:kt + 1], in1=xhi[:, kt, 0:T], op0=ALU.mult,
                        op1=ALU.subtract).then_inc(x_ready, 1)

            nc.vector.memset(eps_t[:], EPS).then_inc(setup, 1)
            own(nc.vector.memset(ones[:], 1.0))
            dve.wait_ge(n_ss, 8)
            nc.vector.tensor_reduce(ss[:, 0:2], sq[:, 0], AX.X, ALU.add).then_inc(n_sum, 1)
            norm(0, x_nat, mix_w, 0)
            for k in range(LEAD):
                split_lo(C_IN, k)

            def start_small():
                dve.wait_ge(c_in, 16 * N_CONST)
                own(tt(lbs[:, 0], lbt[:, 0], lbt[:, 1], ALU.max))
                own(tt(lbt[:, 0], lbt[:, 0], lbs[:, 0], ALU.subtract))
                tt(lbt[:, 1], lbt[:, 1], lbs[:, 0], ALU.subtract).then_inc(lb_max, 1)
                own(tt(lamv[:, 0], lamv[:, 0], lamv[:, 1], ALU.mult))
                own(tt(lamv[:, 2], lamv[:, 2], lamv[:, 3], ALU.mult))
                nc.vector.tensor_reduce(lams[:, 0:2], lamv[:, 0:4:2, :], AX.X, ALU.add).then_inc(lam_sum, 1)
                own(ts(subg[:], gvec[:, 3:4], 1.0 - LAMBDA_INIT, None, ALU.mult))

            def start_meta():
                dve.wait_ge(m_sd, 1)
                own(nc.vector.reciprocal(rstd[0:META, 8:9], ss[0:META, 8:9]))
                ts(meta_nat[:], meta_nat[:], rstd[0:META, 8:9], None, ALU.mult).then_inc(m_un, 1)
                dve.wait_ge(lb_exp, 1)
                own(tt(lbs[:, 1], lbe[:, 0], lbe[:, 1], ALU.add))
                own(nc.vector.reciprocal(lbs[:, 1], lbs[:, 1]))
                own(tt(lbs[:, 2], lbe[:, 0], lbs[:, 1], ALU.mult))
                own(ts(lbs[:, 3], lbs[:, 2], -1.0, 1.0, ALU.mult, ALU.add))
                dve.wait_ge(lam_exp, 1)
                own(tt(lams[:, 4:5], lams[:, 3:4], lams[:, 2:3], ALU.subtract))
                own(ts(lams[:, 5:6], lams[:, 4:5], -LAMBDA_INIT, None, ALU.add))

            def meta_weights():
                dve.wait_ge(m_tr, 1)
                tt(meta_t[:], ps[:, 3, 0:KT * META].rearrange("p (k m) -> p k m", k=KT),
                   spread(pre_w[:], [1, KT], [0, META]), ALU.mult).then_inc(m_w, 1)

            def meta_lower():
                dve.wait_ge(m_hi, 1)
                tt(xlo[:, :, T:TM], meta_t[:], xhi[:, :, T:TM], ALU.subtract).then_inc(meta_ready, 1)

            def evac_in(g):
                s, half = g % 2, slice(4 * (g % 2), 4 * (g % 2) + 4)
                if g not in E_STEP:
                    return
                dve.wait_ge(e_sig, E_STEP[g] + 1)
                if g < 2:
                    stt(out=qp[:, half, :], in0=pset(s), scalar=P ** -0.5, in1=qp[:, half, :], op0=ALU.mult,
                        op1=ALU.mult).then_inc(set_free[s], 1)
                elif g < 4:
                    gg = g_even[:].rearrange("p (n t) -> p n t", t=T)[:, half, :]
                    for b in range(4):
                        hd = 4 * s + b
                        ins = ts(gg[:, b, :], gg[:, b, :], lbs[:, 3, hd:hd + 1], lbs[:, 2, hd:hd + 1], ALU.mult, ALU.add)
                    own(ins)
                    ts(kr[:, half, :], gg, -1.0, 1.0, ALU.mult, ALU.add).then_inc(set_free[s], 1)
                else:
                    stt(out=sg[:, half, :], in0=pset(s), scalar=gvec[:, 0:1], in1=sg[:, half, :], op0=ALU.mult,
                        op1=ALU.mult).then_inc(set_free[s], 1)

            def level_mask(level, i):
                if i == 0:
                    dve.wait_ge(hg_s, level + 1)
                half = slice(8 * i, 8 * i + 8)
                if level == LEVELS - 1:
                    nc.vector.tensor_copy(cross[:, 4 * i:4 * i + 4, :],
                                          misc[:, i, :].rearrange("p (x c) -> p x c", x=4)).then_inc(hg_m, 1)
                    return
                src = misc[:, 2 * i:2 * i + 2, :].rearrange("p b (x c) -> p (b x) c", x=4)
                if level == 0 and i == 0:
                    dve.wait_ge(mask_in, 16)
                if level >= 2:
                    dve.wait_ge(hg_acc, 2 * (level - 2) + i + 1)
                dst = acc if level == 0 else masked
                tt(dst[:, half, :], src, spread(masks[:, level, :], [0, 8], [1, P]), ALU.mult).then_inc(hg_m, 1)

            def q_decay(level):
                flat = qp[:].rearrange("p n t -> p (n t)")
                if level == 0:
                    tt(flat, flat, g_even[:], ALU.mult).then_inc(hg_q, 1)
                    return
                hb = 2 ** (level - 1)
                n = HG * T // (2 * hb)
                src = (g_even, g_odd)[(level - 1) % 2]
                if level >= 2:
                    dve.wait_ge(hg_g, level - 1)
                v = flat.rearrange("p (n two h) -> p n two h", two=2, h=hb)[:, :, 1, :]
                tt(v, v, spread(src[:, 0:1], [2, n], [0, hb]), ALU.mult).then_inc(hg_q, 1)

            def hg_inverse(i):
                dve.wait_ge(hg_sd, i + 1)
                nc.vector.reciprocal(rs_hg[:, 2 * i:2 * i + 2, :], rs_hg[:, 2 * i:2 * i + 2, :]).then_inc(hg_rs, 1)

            def hg_scale(i):
                dve.wait_ge(hg_t, i // 2 + 1)
                dve.wait_ge(hg_rs, i + 1)
                tt(o_hg[:, 2 * i:2 * i + 2, :], o_hg[:, 2 * i:2 * i + 2, :], rs_hg[:, 2 * i:2 * i + 2, :],
                   ALU.mult).then_inc(hg_y, 1)

            def hg_lower(i):
                dve.wait_ge(hg_hi, i + 1)
                tt(ya_lo[:, 2 * i:2 * i + 2, :], o_hg[:, 2 * i:2 * i + 2, :], ya_hi[:, 2 * i:2 * i + 2, :],
                   ALU.subtract).then_inc(ya_ready, 1)

            def att_bias(u):
                dve.wait_ge(at_s, u + 1)
                if u % 2 == 0:
                    dve.wait_ge(rel_ready, u // 2 + 1)
                if u >= 3:
                    dve.wait_ge(at_t, u - 2)
                rb = rel[:, (u // 2) % 2, u % 2, :]
                stt(out=prob[:, u % 3, 0:P], in0=ps[:, 4, 0:P], scalar=-1.0, in1=rb[:, 0:P][:, ::-1], op0=ALU.mult,
                    op1=ALU.subtract)
                own(stt(out=prob[:, u % 3, P:3 * P], in0=ps[:, 4, P:3 * P], scalar=-1.0, in1=rb[:, ::-1], op0=ALU.mult,
                        op1=ALU.subtract))
                own(nc.vector.tensor_reduce(nm[:, u % 3, 0:1], prob[:, u % 3, 0:P], AX.X, ALU.min))
                nc.vector.tensor_reduce(nm[:, u % 3, 1:2], prob[:, u % 3, P:3 * P], AX.X, ALU.min).then_inc(at_nm, 1)

            def att_inverse(u):
                dve.wait_ge(at_exp, 2 * (u + 1))
                own(nc.vector.reciprocal(rinv[:, u % 3, :], rsum[:, u % 3, :]))
                for t, cols in enumerate((slice(0, P), slice(P, 3 * P))):
                    ts(prob[:, u % 3, cols], prob[:, u % 3, cols], rinv[:, u % 3, t:t + 1], None,
                       ALU.mult).then_inc(at_p, 1)

            def att_lower(j):
                dve.wait_ge(at_hi, j + 1)
                tt(yb_lo[:, j, :], ps[:, 6 + j % 2, 0:T], yb_hi[:, j, :], ALU.subtract).then_inc(at_y, 1)

            for g in range(G_IN):
                for k in range(NC):
                    split_lo(C_IN + NC * g, LEAD + k)
                    if G_LEVEL <= g < G_HGOUT:
                        level = g - G_LEVEL
                        if k in (2, 3):
                            level_mask(level, k - 2)
                        if k == 4 and level < LEVELS - 1:
                            q_decay(level)
                    if g == 0 and k in (1, 3, 5, 7):
                        (start_small, start_meta, meta_weights, meta_lower)[k // 2]()
                    if g == G_HGOUT + 1 and k % 2 == 0:
                        hg_inverse(k // 2)
                    if g == G_HGOUT + 2 and k % 2 == 1:
                        hg_scale(k // 2)
                    if g == G_HGOUT + 3 and k % 2 == 1:
                        hg_lower(k // 2)
                    slot, odd = divmod(NC * (g - G_ATT) + k, 2)
                    if g >= G_ATT and not odd:
                        if 1 <= slot < AH + 1:
                            att_inverse(slot - 1)
                        if slot < AH:
                            att_bias(slot)
                    if g >= G_ATT and odd and slot < AH + 3 and slot >= 4 and slot % 2 == 0:
                        att_lower((slot - 4) // 2)
                evac_in(g)

            with dve.Fori(0, 4) as n:
                c0 = C_BR + NC * n
                for k in range(4):
                    split_lo(c0, LEAD + k)
                dve.wait_ge(pe_done, c0 + 4)
                tt(part_a[:], pset(0), gates[:, bass.ds(4 * n, 4), :], ALU.mult).then_inc(set_free[0], 1)
                for k in range(4, 8):
                    split_lo(c0, LEAD + k)
                dve.wait_ge(pe_done, c0 + 8)
                tt(part_b[:], pset(1), gates[:, bass.ds(4 * n + 16, 4), :], ALU.mult).then_inc(set_free[1], 1)
                dve.wait_ge(br_hi, n + 1)
                tt(xlo[:, bass.ds(4 * n, 4), 0:T], both[:], xhi[:, bass.ds(4 * n, 4), 0:T],
                   ALU.subtract).then_inc(br_ready, 1)
            dve.wait_ge(h_in, 16)
            with dve.Fori(0, 2) as i:
                for s in range(2):
                    c0 = C_OUT + 2 * NC * i + NC * s
                    for k in range(NC):
                        split_lo(c0, LEAD + k)
                    dve.wait_ge(pe_done, c0 + NC)
                    hv = h[:, :, bass.ds(2 * CW * i + CW * s, CW)]
                    tt(hv, hv, ps[:, 2 * s:2 * s + 2, :], ALU.add).then_inc(set_free[s], 1)
            dve.wait_ge(n_ss, 16)
            nc.vector.tensor_reduce(ss[:, 2:4], sq[:, 1], AX.X, ALU.add).then_inc(n_sum, 1)
            norm(1, h, mlp_w, 2)

            def quarter(q, last):
                c0 = C_FF + 8 * NC * q
                for g in range(4):
                    for k in range(NC):
                        split_lo(c0 + NC * g, LEAD + k)
                    dve.wait_ge(up_hi, 4 * q + g + 1)
                    dh, dl = ((ya_hi, ya_lo), (yb_hi, yb_lo))[g // 2]
                    bs = slice(4 * (g % 2), 4 * (g % 2) + 4)
                    tt(dl[:, bs, :], relu2[:], dh[:, bs, :], ALU.subtract).then_inc(up_ready, 1)
                for g in range(4):
                    for k in range(NC):
                        split_lo(c0 + 4 * NC + NC * g, LEAD + k)
                    dve.wait_ge(pe_done, c0 + 4 * NC + NC * (g + 1))
                    hv = h[:, :, g * CW:(g + 1) * CW]
                    tt(hv, hv, ps[:, 2 * (g % 2):2 * (g % 2) + 2, :], ALU.add).then_inc(set_free[g % 2], 1)
                    if last:
                        if g == 0:
                            dve.wait_ge(finw_in, 16)
                        dve.wait_ge(f_sq, 2 * (g + 1))
                        tt(hv, hv, spread(fin_w[:, g * CW:(g + 1) * CW], [0, NT], [1, CW]), ALU.mult).then_inc(f_w, 1)

            with dve.Fori(0, QUARTERS - 1) as q:
                quarter(q, False)
            quarter(QUARTERS - 1, True)
            nc.vector.tensor_reduce(ss[:, 4:6], sq[:, 1], AX.X, ALU.add).then_inc(f_un, 1)
            dve.wait_ge(n_ss, 24)
            own(nc.vector.tensor_reduce(ss[:, 6:8], sq[:, 2], AX.X, ALU.add))
            dve.wait_ge(f_un, 2)
            own(nc.vector.reciprocal(rstd[:, 4:6], ss[:, 4:6]))
            own(tt(ss[:, 6:8], ss[:, 6:8], rstd[:, 4:6], ALU.mult))
            tt(ss[:, 6:8], ss[:, 6:8], rstd[:, 4:6], ALU.mult).then_inc(n_sum, 1)
            dve.wait_ge(n_sd, 3)
            own(nc.vector.reciprocal(rstd[:, 12:14], ss[:, 6:8]))
            tt(rstd[:, 6:8], rstd[:, 12:14], rstd[:, 4:6], ALU.mult).then_inc(n_rs, 1)
            norm_tail(2, h, pre_w, 6)

            def values_copy(b):
                dve.wait_ge(vt_t[0], b // 2 + 1)
                nc.vector.tensor_copy(v_nat[:, b, :, :], ps[:, 4 + b % 4, 0:T].rearrange("p (t c) -> p t c", t=2))
                nc.vector.tensor_copy(v_meta[:, b, :], ps[0:META, 4 + b % 4, T:T + P]).then_inc(vt_c[0], 1)

            def rope_inverse(n, i):
                dve.wait_ge(nr_sd, n + 1)
                v = qsq[:, i:i + 1, :] if n == 0 else qsq[:, 2 * i:2 * i + 2, 0:T]
                nc.vector.reciprocal(v, v).then_inc(nr_rs, 1)

            def rope_sin(n, s):
                dve.wait_ge(nr_rot, n + 1)
                if n == 0:
                    tt(qrot[:, 0:2, :], ps[:, 2 * s:2 * s + 2, 0:TM], spread(sin_t[:], [0, 2], [1, TM]),
                       ALU.mult).then_inc(set_free[s], 1)
                else:
                    tt(qrot[:, :, 0:T], pset(s), spread(sin_t[:], [0, 4], [1, T]), ALU.mult).then_inc(set_free[s], 1)

            def evac_in2(j):
                if j < 9:
                    return
                g = j - 9
                s, half = g % 2, slice(4 * (g % 2), 4 * (g % 2) + 4)
                dve.wait_ge(e_sig, N_E1 + g + 1)
                dst = (gb if g < 2 else ga)[:, half, :]
                stt(out=dst, in0=pset(s), scalar=subg[:] if g < 2 else 1.0, in1=dst, op0=ALU.mult,
                    op1=ALU.mult).then_inc(set_free[s], 1)

            def unit_max(u):
                hd, t = divmod(u % B_UNITS, NT)
                dve.wait_ge(u_s, u + 1)
                if u >= 4:
                    dve.wait_ge(u_t, u - 3)
                if u < B_UNITS:
                    own(stt(out=p2[:, u % 4, :, :], in0=spread(dist[:, t, :], [0, 2], [1, TM]),
                            scalar=float(2.0 ** (-8.0 * (hd + 1.0) / H2)), in1=ps[:, 4:6, 0:TM], op0=ALU.mult,
                            op1=ALU.subtract))
                    nc.vector.tensor_reduce(nm[:, u % 4, :], p2[:, u % 4, :, :], AX.X, ALU.min).then_inc(u_nm, 1)
                else:
                    own(nc.vector.tensor_reduce(nm[:, u % 4, 1:2], ps[:, 4 + u % 2, 0:TM], AX.X, ALU.max))
                    ts(nm[:, u % 4, 0:1], nm[:, u % 4, 1:2], -P ** -0.5, None, ALU.mult).then_inc(u_nm, 1)

            def unit_norm(u):
                dve.wait_ge(u_exp, u + 1)
                p, ri = p2[:, u % 4], rinv[:, u % 4]
                if u < B_UNITS:
                    own(nc.vector.reciprocal(ri, rsum[:, u % 4, :]))
                    own(ts(ri[:, 1:2], ri[:, 1:2], lams[:, 5:6], None, ALU.mult))
                    own(ts(p[:, 0], p[:, 0], ri[:, 0:1], None, ALU.mult))
                    stt(out=p[:, 0], in0=p[:, 1], scalar=ri[:, 1:2], in1=p[:, 0], op0=ALU.mult,
                        op1=ALU.add).then_inc(u_p, 1)
                else:
                    own(nc.vector.reciprocal(ri[:, 0:1], rsum[:, u % 4, 0:1]))
                    ts(p[:, 0], p[:, 0], ri[:, 0:1], None, ALU.mult).then_inc(u_p, 1)

            def unit_out(u):
                dve.wait_ge(u_pv, u + 1)
                hd, t = divmod(u % B_UNITS, NT)
                dst = ob if u < B_UNITS else oa
                nc.vector.tensor_copy(dst[:, hd, t * P:(t + 1) * P], ps[:, 7, 0:P]).then_inc(u_o, 1)

            def side(pos):
                if unit_at(pos - 4) is not None:
                    unit_out(unit_at(pos - 4))
                if unit_at(pos - 2) is not None:
                    unit_norm(unit_at(pos - 2))
                if unit_at(pos) is not None:
                    unit_max(unit_at(pos))
                if POS_BN + 1 < pos <= POS_BN + 5:
                    i = pos - POS_BN - 2
                    dve.wait_ge(bn_sd, i + 1)
                    nc.vector.reciprocal(obr[:, 2 * i:2 * i + 2, :], obr[:, 2 * i:2 * i + 2, :]).then_inc(bn_rs, 1)

            def y_lower(mixer, i, src, upper, ready):
                dve.wait_ge(upper, i + 1)
                tt(yt_lo[mixer][:, 4 * i:4 * i + 4, :], src[:, 4 * i:4 * i + 4, :],
                   yt_hi[mixer][:, 4 * i:4 * i + 4, :], ALU.subtract).then_inc(ready, 1)

            for j in range(G_IN2):
                for k in range(NC):
                    split_lo(C_IN2 + NC * j, LEAD + k)
                    if j == 0 and k in (2, 4):
                        t = k // 2 - 1
                        dve.wait_ge(n_un1, 12)
                        ts(h[:, t], h[:, t], rstd[:, 4 + t:5 + t], None, ALU.mult).then_inc(h_ready, 1)
                    if j == 5 and 2 <= k <= 6:
                        values_copy(2 * (k - 2))
                    for n, jn in enumerate((5, 8, 9)):
                        if j == jn and k in (3, 4):
                            rope_inverse(n, k - 3)
                        if j == jn and k == 5:
                            rope_sin(n, (1, 0, 1)[n])
                    if j >= J_B:
                        side(NC * (j - J_B) + k)
                    if j == G_IN2 - 1 and k in (2, 4):
                        y_lower(1, k // 2 - 1, ob, bn_hi, yb2_ready)
                    if j == G_IN2 - 1 and k == 6:
                        y_lower(0, 0, oa, an_hi, ya2_ready)
                evac_in2(j)
            y_lower(0, 1, oa, an_hi, ya2_ready)

            dve.wait_ge(postw_in, 16)
            for g in range(4):
                for k in range(NC):
                    if NC * g + LEAD + k < 4 * NC:
                        split_lo(C_OUT2 + NC * g, LEAD + k)
                cols = slice(g * CW, (g + 1) * CW)
                dve.wait_ge(pe_done, C_OUT2 + NC * (g + 1))
                tt(y2[:, 1, cols], ps[:, 2 * (g % 2) + 1, :], post_w[:, cols], ALU.mult).then_inc(y_w, 1)
                dve.wait_ge(y_ss, 2 * g + 2 if g < 2 else 2 * g + 1)
                tt(y2[:, 0, cols], ps[:, 2 * (g % 2), :], post_w[:, cols], ALU.mult).then_inc(set_free[g % 2], 1)
            dve.wait_ge(y_ss, 8)
            nc.vector.tensor_reduce(ss[:, 10:12], sq[:, 0], AX.X, ALU.add).then_inc(y_sd, 1)
            dve.wait_ge(y_sd, 2)
            own(nc.vector.reciprocal(rstd[:, 10:12], ss[:, 10:12]))
            dve.wait_ge(h_ready, NT)
            for i in range(2 * NT):
                t, cols = i // 2, slice((i % 2) * (D // 2), (i % 2 + 1) * (D // 2))
                stt(out=y2[:, t, cols], in0=y2[:, t, cols], scalar=rstd[:, 10 + t:11 + t], in1=h[:, t, cols],
                    op0=ALU.mult, op1=ALU.add).then_inc(y_out, 1)

        @block.gpsimd
        def _(pool):
            tt = nc.gpsimd.tensor_tensor

            def load(dst, src):
                return pool.dma_start(dst, src, allow_slow_non_contiguous=True)

            load(mix_w[:], norm_mix_w[0].rearrange("(k p) -> p k", p=P)).then_inc(mixw_in, 16)
            small = [
                (lbt[:, 0], lb_logits[0].rearrange("(k p) -> p k", p=P)),
                (lbt[:, 1], lb_logits[1].rearrange("(k p) -> p k", p=P)),
                (gvec[:, 0:1], hg_norm_w[0].rearrange("(p k) -> p k", k=1)),
                (gvec[:, 1:2], q_norm_g_2[0].rearrange("(p k) -> p k", k=1)),
                (gvec[:, 2:3], k_norm_g_2[0].rearrange("(p k) -> p k", k=1)),
                (gvec[:, 3:4], subln_g_2[0].rearrange("(p k) -> p k", k=1)),
                (lamv[:, 0], row_all(lambda_q1_2, DH)), (lamv[:, 1], row_all(lambda_k1_2, DH)),
                (lamv[:, 2], row_all(lambda_q2_2, DH)), (lamv[:, 3], row_all(lambda_k2_2, DH)),
                (mlp_w[:], norm_mlp_w[0].rearrange("(k p) -> p k", p=P)),
                (pre_w[:], pre_norm_g_2[0].rearrange("(k p) -> p k", p=P)),
                (cos_t[:], rope_cos), (sin_t[:], rope_sin), (turn[:], rope_turn),
                (dist[:], distance.rearrange("(t p) k -> p t k", p=P)),
            ]
            assert len(small) == N_CONST
            load(meta_nat[:], meta_tokens_2).then_inc(meta_in, 16)
            for dst, src in small:
                load(dst, src).then_inc(c_in, 16)
            load(masks[:], level_masks).then_inc(mask_in, 16)

            def level_add(level, i):
                pool.wait_ge(hg_m, 2 * level + i + 1)
                half = slice(8 * i, 8 * i + 8)
                tt(acc[:, half, :], acc[:, half, :], masked[:, half, :], ALU.add).then_inc(hg_acc, 1)

            def k_decay(level):
                hb = 2 ** (level - 1)
                n = HG * T // (2 * hb)
                src, dst = (g_even, g_odd)[(level - 1) % 2], (g_even, g_odd)[level % 2]
                pool.wait_ge(hg_s, level + 1)
                if level >= 2:
                    pool.wait_ge(hg_g, level - 1)
                pool.wait_ge(hg_q, level)
                pair = src[:, 0:2 * n].rearrange("p (n two) -> p n two", two=2)
                if level < LEVELS - 2:
                    tt(dst[:, 0:n], pair[:, :, 0], pair[:, :, 1], ALU.mult).then_inc(hg_g, 1)
                v = kr[:].rearrange("p n t -> p (n t)").rearrange("p (n two h) -> p n two h", two=2, h=hb)[:, :, 0, :]
                tt(v, v, spread(src[:, 1:2], [2, n], [0, hb]), ALU.mult).then_inc(hg_k, 1)

            def bias_load(j):
                if j == 0:
                    pool.wait_ge(hg_m, 2 * LEVELS)
                if j >= 2:
                    pool.wait_ge(at_nm, 2 * (j - 1))
                src = bass.AP(rel_bias.tensor, rel_bias.offset + 2 * j * N_REL + REL_CLIP + P - (T - 1),
                              [[1, P], [N_REL, 2], [1, T]])
                load(rel[:, j % 2, :, :], src).then_inc(rel_in[j % 2], 16)
                pool.wait_ge(rel_in[j % 2], 16 * (j // 2 + 1))
                nc.gpsimd.memset(rel[0:DH, j % 2, :, 0:DH], MASKED).then_inc(rel_ready, 1)

            for g in range(G_IN):
                if G_LEVEL < g < G_HGOUT - 1:
                    level = g - G_LEVEL
                    for i in range(2):
                        level_add(level, i)
                    k_decay(level)
                if g == G_HGOUT:
                    for i in range(4):
                        pool.wait_ge(hg_os, i + 1)
                        tt(o2_hg[:, 2 * i:2 * i + 2, :], o_hg[:, 2 * i:2 * i + 2, :], o_hg[:, 2 * i:2 * i + 2, :],
                           ALU.mult).then_inc(hg_o2, 1)
                if g == G_HGOUT + 1:
                    pool.wait_ge(hg_o2, 4)
                    for i in range(2):
                        tt(o_hg[:, 4 * i:4 * i + 4, :], o_hg[:, 4 * i:4 * i + 4, :], sg[:, 4 * i:4 * i + 4, :],
                           ALU.mult).then_inc(hg_t, 1)
                    bias_load(0)
                if g >= G_ATT:
                    for k in range(NC):
                        slot, odd = divmod(NC * (g - G_ATT) + k, 2)
                        if not odd and slot < AH and slot % 2 == 0 and slot // 2 + 1 < AH // 2:
                            bias_load(slot // 2 + 1)

            with pool.Fori(0, 4) as n:
                pool.wait_ge(set_free[1], G_IN // 2 + n + 1)
                tt(both[:], part_a[:], part_b[:], ALU.add).then_inc(br_m, 1)
            pool.wait_ge(br_ready, 4)
            load(fin_w[:], row_all(norm_final_w, D)).then_inc(finw_in, 16)
            with pool.Fori(0, QUARTERS) as q:
                for g in range(4):
                    pool.wait_ge(set_free[g % 2], G_IN // 2 + 6 + 4 * q + g // 2 + 1)
                    tt(relu2[:], relu[:], relu[:], ALU.mult).then_inc(up_sq, 1)

            def rope(n):
                pool.wait_ge(nr_rot, n + 1)
                w = TM if n == 0 else T
                nb = 2 if n == 0 else 4
                dst = ka[:] if n == 0 else qa[:, 4 * (n - 1):4 * n, :]
                v, r, q = qg[:, 0:nb, 0:w], qrot[:, 0:nb, 0:w], qsq[:, 0:nb, 0:w]
                tt(v, v, spread(cos_t[:], [0, nb], [1, w]), ALU.mult).then_inc(nr_cos, 1)
                pool.wait_ge(nr_cos, 2 * n + 1)
                pool.wait_ge(set_free[(1, 0, 1)[n]], rope_free[n])
                tt(v, v, r, ALU.add).then_inc(nr_cos, 1)
                pool.wait_ge(nr_cos, 2 * n + 2)
                pool.wait_ge(nr_rs, 2 * (n + 1))
                tt(dst, v, q, ALU.mult).then_inc(nr_done, 1)

            rope_free = (SETS_BEFORE_2 + 4, need2[7] + 1, need2[8] + 1)
            rope(0)
            pool.wait_ge(u_o, B_UNITS)
            tt(ob2[:], ob[:], ob[:], ALU.mult).then_inc(bn_o2, 1)
            rope(1)
            rope(2)
            for i in range(2):
                v, half = ob[:, 4 * i:4 * i + 4, :], slice(4 * i, 4 * i + 4)
                pool.wait_ge(bn_rs, 2 * (i + 1))
                tt(v, v, obr[:, half, :], ALU.mult).then_inc(bn_n, 1)
                pool.wait_ge(bn_n, i + 1)
                pool.wait_ge(set_free[i], need2[9 + i] + 1)
                tt(v, v, gb[:, half, :], ALU.mult).then_inc(bn_y, 1)
            pool.wait_ge(bn_y, 2)
            load(post_w[:], row_all(post_norm_g_2, D)).then_inc(postw_in, 16)
            for i in range(2):
                v, half = oa[:, 4 * i:4 * i + 4, :], slice(4 * i, 4 * i + 4)
                pool.wait_ge(u_o, B_UNITS + B_UNITS // 2 * (i + 1))
                pool.wait_ge(set_free[i], need2[11 + i] + 1)
                tt(v, v, ga[:, half, :], ALU.mult).then_inc(an_y, 1)


_NAMES = ("x", "w_in", "lb_logits", "hg_norm_w", "rel_bias", "w_branch_a", "w_branch_b", "w_out", "norm_mix_w",
          "norm_mlp_w", "w_up", "w_down", "norm_final_w", "meta_tokens_2", "pre_norm_g_2", "w_in_2", "q_norm_g_2",
          "k_norm_g_2", "lambda_q1_2", "lambda_k1_2", "lambda_q2_2", "lambda_k2_2", "subln_g_2", "w_out_2",
          "post_norm_g_2")


def shape_constants():
    f32 = np.float32
    identity = np.eye(P, dtype=f32)
    s, t = np.arange(P)[:, None], np.arange(P)[None, :]
    masks = np.zeros((P, 8, P), f32)
    masks[:, 0, :] = s == t
    for level in range(1, 8):
        hb = 2 ** (level - 1)
        masks[:, level, :] = (s // (2 * hb) == t // (2 * hb)) & ((s // hb) % 2 == 0) & ((t // hb) % 2 == 1)
    inv_freq = (f32(10000.0) ** (-np.arange(0, DH, 2, dtype=f32) / f32(DH))).astype(f32)
    row = np.concatenate([np.arange(T) // 64, np.zeros(META, int)]).astype(f32)
    col = np.concatenate([np.arange(T) % 64, np.zeros(META, int)]).astype(f32)
    ang = np.stack([row[:, None] * inv_freq, col[:, None] * inv_freq]).astype(f32)
    half = np.concatenate([ang[0], ang[0], ang[1], ang[1]], axis=1).T
    rope_cos, rope_sin = np.cos(half).astype(f32), np.sin(half).astype(f32)
    turn = np.zeros((P, P), f32)
    for m in range(P):
        if (m // 32) % 2 == 0:
            turn[m + 32, m] = -1.0
        else:
            turn[m - 32, m] = 1.0
    qpos = np.arange(T) + META
    kpos = np.concatenate([np.arange(T) + META, np.arange(META)])
    distance = np.abs(qpos[:, None] - kpos[None, :]).astype(f32)
    return {"identity": identity, "level_masks": masks, "rope_cos": rope_cos, "rope_sin": rope_sin,
            "rope_turn": turn, "distance": distance}


def kernel(**inputs):
    import concourse.bacc as bacc
    from concourse.bass_utils import run_bass_kernel_spmd

    nc = bacc.Bacc("TRN2", target_bir_lowering=False, num_devices=1)
    arrays, args = {}, []
    for name, a in [(n, inputs[n]) for n in _NAMES] + list(shape_constants().items()):
        a = np.ascontiguousarray(a)
        arrays[f"in_{name}_dram"] = a
        args.append(nc.dram_tensor(f"in_{name}_dram", a.shape, mybir.dt.from_np(a.dtype), kind="ExternalInput").ap())
    out = nc.dram_tensor("out_0_dram", (1, T, D), F32, kind="ExternalOutput").ap()
    program(nc, *args, out)
    r = run_bass_kernel_spmd(nc, [arrays], core_ids=[0])
    return r.results[0]["out_0_dram"]
```
